# Optimizing a Trainium2 kernel written in Bass

```python
import jax, jax.numpy as jnp
from jax import lax
import numpy as np
import math

D_MODEL = 1024
BATCH = 1
SEQ = 256
DEPTH = 1

N_META = 16
POOL_WIDTH = D_MODEL // 2
POOL_WINDOWS = (2, 4, 8, 16)
POOL_GROUP = POOL_WIDTH // len(POOL_WINDOWS)
N_HEADS = 8
HEAD_DIM = 64
ATTN_WIDTH = N_HEADS * HEAD_DIM
Q_BLOCK = 128
RMS_EPS = 1e-6
IN_SIZES = (POOL_WIDTH, POOL_WIDTH, ATTN_WIDTH, ATTN_WIDTH, ATTN_WIDTH, ATTN_WIDTH, N_HEADS, D_MODEL, D_MODEL)
N_IN = 2 * POOL_WIDTH + 4 * ATTN_WIDTH + N_HEADS + 2 * D_MODEL


def _split_points():
    pts, acc = [], 0
    for s in IN_SIZES[:-1]:
        acc += s
        pts.append(acc)
    return pts

def rmsnorm(x, g):
    xf = x.astype(jnp.float32)
    xf = xf * lax.rsqrt(jnp.mean(xf * xf, axis=-1, keepdims=True) + RMS_EPS)
    return (xf * g.astype(jnp.float32)).astype(x.dtype)

def causal_multiscale_pool(u, pool_w, pool_scale):
    B, L, _ = u.shape
    groups = jnp.split(u, len(POOL_WINDOWS), axis=-1)
    pos = jnp.arange(L, dtype=jnp.float32)[:, None]
    pooled = []
    for w, ug in zip(POOL_WINDOWS, groups):
        uf = ug.astype(jnp.float32)
        c = jnp.cumsum(uf, axis=1)
        c_prev = jnp.pad(c, ((0, 0), (w, 0), (0, 0)))[:, :L]
        count = jnp.minimum(pos + 1.0, float(w))
        pooled.append((c - c_prev) / count - uf)
    p = jnp.stack(pooled, axis=2).astype(u.dtype)
    y = jnp.einsum('blgc,gcd->blgd', p, pool_w)
    return y.reshape(B, L, POOL_WIDTH) * pool_scale

def forgetting_attention(q, k, v, log_f):
    B, L, H, Dh = q.shape
    pad = (Q_BLOCK - L % Q_BLOCK) % Q_BLOCK
    padw = ((0, 0), (pad, 0), (0, 0), (0, 0))
    qp, kp, vp = jnp.pad(q, padw), jnp.pad(k, padw), jnp.pad(v, padw)
    c = jnp.cumsum(log_f, axis=1)
    c = jnp.transpose(jnp.pad(c, ((0, 0), (pad, 0), (0, 0))), (0, 2, 1))
    Lp = L + pad
    scale = 1.0 / np.sqrt(HEAD_DIM)
    outs = []
    for i in range(Lp // Q_BLOCK):
        q0, q1 = i * Q_BLOCK, (i + 1) * Q_BLOCK
        qb, kb, vb = qp[:, q0:q1], kp[:, :q1], vp[:, :q1]
        s = jnp.einsum('bqhd,bkhd->bhqk', qb, kb).astype(jnp.float32) * scale
        s = s + c[:, :, q0:q1, None] - c[:, :, None, :q1]
        q_idx = jnp.arange(q0, q1)[:, None]
        k_idx = jnp.arange(q1)[None, :]
        valid = (k_idx <= q_idx) & ((k_idx >= pad) | (k_idx == q_idx))
        s = jnp.where(valid, s, -jnp.inf)
        p = jax.nn.softmax(s, axis=-1)
        outs.append(jnp.einsum('bhqk,bkhd->bqhd', p.astype(vb.dtype), vb))
    o = jnp.concatenate(outs, axis=1)[:, pad:]
    return o

def hybrid_layer(x, norm_g, w_in, b_forget, pool_w, pool_scale, w_up_pool, w_up_attn, w_out):
    B, L, _ = x.shape
    h = rmsnorm(x, norm_g)
    proj = jnp.einsum('bld,dn->bln', h, w_in)
    u_pool, z_pool, q, k, v, z_attn, f_logit, g_pool, g_attn = jnp.split(proj, _split_points(), axis=-1)
    y_pool = causal_multiscale_pool(u_pool, pool_w, pool_scale) * jax.nn.silu(z_pool)
    q = q.reshape(B, L, N_HEADS, HEAD_DIM)
    k = k.reshape(B, L, N_HEADS, HEAD_DIM)
    v = v.reshape(B, L, N_HEADS, HEAD_DIM)
    log_f = jax.nn.log_sigmoid((f_logit + b_forget).astype(jnp.float32))
    y_attn = forgetting_attention(q, k, v, log_f).reshape(B, L, ATTN_WIDTH) * jax.nn.silu(z_attn)
    merged = (jax.nn.sigmoid(g_pool) * jnp.einsum('blc,cd->bld', y_pool, w_up_pool)
              + jax.nn.sigmoid(g_attn) * jnp.einsum('blc,cd->bld', y_attn, w_up_attn))
    return x + jnp.einsum('bld,de->ble', merged, w_out)

def first_inputs(seed: int = 0) -> dict:
    key = jax.random.key(seed)
    ks = jax.random.split(key, 12)
    f0 = sum(IN_SIZES[:6])
    x = jax.random.normal(ks[0], (BATCH, SEQ, D_MODEL), jnp.float32)
    meta_tokens = jax.random.normal(ks[1], (N_META, D_MODEL), jnp.float32)
    norm_g = 1.0 + 0.02 * jax.random.normal(ks[2], (DEPTH, D_MODEL), jnp.float32)
    w_in = jax.random.normal(ks[3], (DEPTH, D_MODEL, N_IN), jnp.float32) * D_MODEL ** -0.5
    w_in = w_in.at[:, :, f0:f0 + N_HEADS].multiply(0.1)
    b_forget = (jnp.linspace(1.0, 6.0, N_HEADS, dtype=jnp.float32)[None, :]
                + 0.1 * jax.random.normal(ks[4], (DEPTH, N_HEADS), jnp.float32))
    pool_w = jax.random.normal(ks[5], (DEPTH, len(POOL_WINDOWS), POOL_GROUP, POOL_GROUP), jnp.float32) * POOL_GROUP ** -0.5
    pool_scale = 1.0 + 0.1 * jax.random.normal(ks[6], (DEPTH, POOL_WIDTH), jnp.float32)
    w_up_pool = jax.random.normal(ks[7], (DEPTH, POOL_WIDTH, D_MODEL), jnp.float32) * POOL_WIDTH ** -0.5
    w_up_attn = jax.random.normal(ks[8], (DEPTH, ATTN_WIDTH, D_MODEL), jnp.float32) * ATTN_WIDTH ** -0.5
    w_out = jax.random.normal(ks[9], (DEPTH, D_MODEL, D_MODEL), jnp.float32) * D_MODEL ** -0.5
    final_norm_g = 1.0 + 0.02 * jax.random.normal(ks[10], (D_MODEL,), jnp.float32)
    return {"x": x, "meta_tokens": meta_tokens, "norm_g": norm_g, "w_in": w_in,
            "b_forget": b_forget, "pool_w": pool_w, "pool_scale": pool_scale,
            "w_up_pool": w_up_pool, "w_up_attn": w_up_attn, "w_out": w_out,
            "final_norm_g": final_norm_g}

def first_block(x, meta_tokens, norm_g, w_in, b_forget, pool_w, pool_scale, w_up_pool, w_up_attn, w_out, final_norm_g):
    B = x.shape[0]
    meta = jnp.broadcast_to(meta_tokens.astype(x.dtype)[None], (B, N_META, D_MODEL))
    h = jnp.concatenate([meta, x], axis=1)
    for l in range(DEPTH):
        h = hybrid_layer(h, norm_g[l], w_in[l], b_forget[l], pool_w[l], pool_scale[l],
                         w_up_pool[l], w_up_attn[l], w_out[l])
    h = rmsnorm(h, final_norm_g)
    return h[:, N_META:]


DEPTH_2 = 2

CHUNK = 64
EPS = 1e-6
N_A_LAYERS = DEPTH_2 // 2
N_B_LAYERS = DEPTH_2 - N_A_LAYERS

A_HEADS = 6
A_HEAD_DIM = 128
A_WIDTH = A_HEADS * A_HEAD_DIM
CONV_K = 4

B_HEADS = 6
QK_NOPE = 128
QK_ROPE = 64
V_HEAD = 128
Q_LORA = 256
KV_LORA = 256
B_WIDTH = B_HEADS * V_HEAD
ROPE_THETA = 10000.0

N_MEM = 256
MEM_HEADS = 4
MEM_HEAD_DIM = 64
MEM_WIDTH = MEM_HEADS * MEM_HEAD_DIM

D_FF = 2816

MIX_WIDTH = A_WIDTH + MEM_WIDTH
A_IN = 4 * A_WIDTH + 2 * A_HEADS + MEM_WIDTH
B_IN = Q_LORA + MEM_WIDTH


def rms_norm(x, g):
    xf = x.astype(jnp.float32)
    y = xf * lax.rsqrt(jnp.mean(xf * xf, axis=-1, keepdims=True) + EPS)
    return (y * g.astype(jnp.float32)).astype(x.dtype)

def l2_norm(x):
    xf = x.astype(jnp.float32)
    return (xf * lax.rsqrt(jnp.sum(xf * xf, axis=-1, keepdims=True) + EPS)).astype(x.dtype)

def swiglu(x, w_gu, w_down):
    gate, up = jnp.split(x @ w_gu, 2, axis=-1)
    return (jax.nn.silu(gate) * up) @ w_down

def rope_tables(positions, dim):
    inv = ROPE_THETA ** (-jnp.arange(0, dim, 2, dtype=jnp.float32) / dim)
    ang = positions.astype(jnp.float32)[..., None] * inv
    return jnp.cos(ang), jnp.sin(ang)

def apply_rope(x, cos, sin):
    xf = x.astype(jnp.float32)
    x1, x2 = jnp.split(xf, 2, axis=-1)
    c, s = cos[:, :, None, :], sin[:, :, None, :]
    return jnp.concatenate([x1 * c - x2 * s, x1 * s + x2 * c], axis=-1).astype(x.dtype)

def causal_depthwise_conv(x, w):
    k = w.shape[0]
    return lax.conv_general_dilated(
        x, w[:, None, :].astype(x.dtype), window_strides=(1,), padding=[(k - 1, 0)],
        dimension_numbers=("NWC", "WIO", "NWC"), feature_group_count=x.shape[-1])

def chunked_gated_delta_rule(q, k, v, beta, g):
    b, s, h, dk = q.shape
    dv = v.shape[-1]
    n = s // CHUNK
    f32 = jnp.float32

    def chunks(t):
        return t.astype(f32).reshape(b, n, CHUNK, h, -1).transpose(0, 3, 1, 2, 4)

    q, k, v = chunks(q), chunks(k), chunks(v)
    beta = chunks(beta[..., None])[..., 0]
    g_cum = jnp.cumsum(chunks(g[..., None])[..., 0], axis=-1)
    causal = jnp.tril(jnp.ones((CHUNK, CHUNK), dtype=bool))
    strict = jnp.tril(jnp.ones((CHUNK, CHUNK), dtype=bool), -1)
    diff = g_cum[..., :, None] - g_cum[..., None, :]
    decay = jnp.where(causal, jnp.exp(jnp.where(causal, diff, 0.0)), 0.0)
    k_beta = k * beta[..., None]
    t_mat = jnp.where(strict, jnp.einsum("bhnid,bhnjd->bhnij", k_beta, k) * decay, 0.0) \
        + jnp.eye(CHUNK, dtype=f32)
    u = lax.linalg.triangular_solve(t_mat, v * beta[..., None], left_side=True,
                                    lower=True, unit_diagonal=True)
    w = lax.linalg.triangular_solve(t_mat, k_beta * jnp.exp(g_cum)[..., None], left_side=True,
                                    lower=True, unit_diagonal=True)
    qk = jnp.einsum("bhnid,bhnjd->bhnij", q, k) * decay
    g_last = g_cum[..., -1:]
    q_dec = q * jnp.exp(g_cum)[..., None]
    k_dec = k * jnp.exp(g_last - g_cum)[..., None]
    chunk_decay = jnp.exp(g_last[..., 0])
    xs = tuple(jnp.moveaxis(t, 2, 0) for t in (q_dec, k_dec, w, u, qk, chunk_decay))

    def step(state, inp):
        q_c, k_c, w_c, u_c, qk_c, d_c = inp
        v_new = u_c - jnp.einsum("bhcd,bhde->bhce", w_c, state)
        out = jnp.einsum("bhcd,bhde->bhce", q_c, state) + jnp.einsum("bhij,bhje->bhie", qk_c, v_new)
        state = state * d_c[..., None, None] + jnp.einsum("bhcd,bhce->bhde", k_c, v_new)
        return state, out

    _, o = lax.scan(step, jnp.zeros((b, h, dk, dv), f32), xs)
    return o.transpose(1, 0, 3, 2, 4).reshape(b, s, h, dv)

def gated_deltanet(qkv, gate, b_raw, a_raw, conv_w, A_log, dt_bias, out_gain):
    b, s, _ = qkv.shape
    qkv = jax.nn.silu(causal_depthwise_conv(qkv, conv_w))
    q, k, v = (t.reshape(b, s, A_HEADS, A_HEAD_DIM) for t in jnp.split(qkv, 3, axis=-1))
    q = l2_norm(q) * A_HEAD_DIM ** -0.5
    k = l2_norm(k)
    beta = jax.nn.sigmoid(b_raw.astype(jnp.float32))
    g = -jnp.exp(A_log.astype(jnp.float32)) * jax.nn.softplus(
        a_raw.astype(jnp.float32) + dt_bias.astype(jnp.float32))
    o = chunked_gated_delta_rule(q, k, v, beta, g).astype(qkv.dtype)
    o = rms_norm(o, out_gain) * jax.nn.silu(gate.reshape(b, s, A_HEADS, A_HEAD_DIM))
    return o.reshape(b, s, A_WIDTH)

def mla_attention(q_nope, q_rope, k_nope, k_rope, v):
    b, s, h, _ = q_nope.shape
    nb = s // Q_BLOCK
    scale = (QK_NOPE + QK_ROPE) ** -0.5
    key_chunk = jnp.arange(s) // CHUNK
    qn = q_nope.reshape(b, nb, Q_BLOCK, h, QK_NOPE).swapaxes(0, 1)
    qr = q_rope.reshape(b, nb, Q_BLOCK, h, QK_ROPE).swapaxes(0, 1)

    def block(args):
        i, qn_b, qr_b = args
        sc = (jnp.einsum("bqhd,bkhd->bhqk", qn_b, k_nope)
              + jnp.einsum("bqhd,bkd->bhqk", qr_b, k_rope)).astype(jnp.float32) * scale
        q_chunk = (i * Q_BLOCK + jnp.arange(Q_BLOCK)) // CHUNK
        mask = key_chunk[None, :] <= q_chunk[:, None]
        p = jax.nn.softmax(jnp.where(mask, sc, -jnp.inf), axis=-1).astype(v.dtype)
        return jnp.einsum("bhqk,bkhd->bqhd", p, v)

    out = lax.map(block, (jnp.arange(nb), qn, qr))
    return out.swapaxes(0, 1).reshape(b, s, h * V_HEAD)

def memory_attention(q, mem_kv):
    b, s, _ = q.shape
    q = q.reshape(b, s, MEM_HEADS, MEM_HEAD_DIM)
    k, v = (t.reshape(b, N_MEM, MEM_HEADS, MEM_HEAD_DIM) for t in jnp.split(mem_kv, 2, axis=-1))
    sc = jnp.einsum("bqhd,bmhd->bhqm", q, k).astype(jnp.float32) * MEM_HEAD_DIM ** -0.5
    p = jax.nn.softmax(sc, axis=-1).astype(v.dtype)
    return jnp.einsum("bhqm,bmhd->bqhd", p, v).reshape(b, s, MEM_WIDTH)

def second_inputs(seed: int = 0) -> dict:
    key = jax.random.key(seed)
    ks = iter(jax.random.split(key, 40))
    f32 = jnp.float32

    def dense(shape, fan_in):
        return jax.random.normal(next(ks), shape, f32) * fan_in ** -0.5

    def gain(shape):
        return 1.0 + 0.02 * jax.random.normal(next(ks), shape, f32)

    x = jax.random.normal(next(ks), (BATCH, SEQ, D_MODEL), f32)
    mem = jax.random.normal(next(ks), (BATCH, N_MEM, D_MODEL), f32)
    offset = jax.random.randint(next(ks), (BATCH, 1), 0, 64, dtype=jnp.int32) * CHUNK
    positions = (offset + jnp.arange(SEQ, dtype=jnp.int32)[None, :]).astype(jnp.int32)

    ffn1_norm = gain((DEPTH_2, D_MODEL))
    ffn1_w_gu = dense((DEPTH_2, D_MODEL, 2 * D_FF), D_MODEL)
    ffn1_w_down = dense((DEPTH_2, D_FF, D_MODEL), D_FF)
    mix_norm = gain((DEPTH_2, D_MODEL))
    ffn2_norm = gain((DEPTH_2, D_MODEL))
    ffn2_w_gu = dense((DEPTH_2, D_MODEL, 2 * D_FF), D_MODEL)
    ffn2_w_down = dense((DEPTH_2, D_FF, D_MODEL), D_FF)
    w_out = dense((DEPTH_2, MIX_WIDTH, D_MODEL), MIX_WIDTH)
    mem_norm = gain((D_MODEL,))
    w_mem_kv = dense((DEPTH_2, D_MODEL, 2 * MEM_WIDTH), D_MODEL)

    a_w_in = dense((N_A_LAYERS, D_MODEL, A_IN), D_MODEL)
    a_conv = dense((N_A_LAYERS, CONV_K, 3 * A_WIDTH), CONV_K)
    a_A_log = jnp.log(jax.random.uniform(next(ks), (N_A_LAYERS, A_HEADS), f32, 1.0, 16.0))
    dt = jnp.exp(jax.random.uniform(next(ks), (N_A_LAYERS, A_HEADS), f32,
                                    math.log(1e-3), math.log(1e-1)))
    a_dt_bias = dt + jnp.log(-jnp.expm1(-dt))
    a_out_norm = gain((N_A_LAYERS, A_HEAD_DIM))

    b_w_in = dense((N_B_LAYERS, D_MODEL, B_IN), D_MODEL)
    b_q_norm = gain((N_B_LAYERS, Q_LORA))
    b_w_uq = dense((N_B_LAYERS, Q_LORA, B_HEADS * (QK_NOPE + QK_ROPE)), Q_LORA)

    kv_in_norm = gain((D_MODEL,))
    w_dkv = dense((D_MODEL, KV_LORA + QK_ROPE), D_MODEL)
    kv_lat_norm = gain((KV_LORA,))
    w_ukv = dense((KV_LORA, B_HEADS * (QK_NOPE + V_HEAD)), KV_LORA)
    final_norm = gain((D_MODEL,))

    return {"x": x, "mem": mem, "positions": positions,
            "ffn1_norm": ffn1_norm, "ffn1_w_gu": ffn1_w_gu, "ffn1_w_down": ffn1_w_down,
            "mix_norm": mix_norm,
            "ffn2_norm": ffn2_norm, "ffn2_w_gu": ffn2_w_gu, "ffn2_w_down": ffn2_w_down,
            "w_out": w_out, "mem_norm": mem_norm, "w_mem_kv": w_mem_kv,
            "a_w_in": a_w_in, "a_conv": a_conv, "a_A_log": a_A_log, "a_dt_bias": a_dt_bias,
            "a_out_norm": a_out_norm,
            "b_w_in": b_w_in, "b_q_norm": b_q_norm, "b_w_uq": b_w_uq,
            "kv_in_norm": kv_in_norm, "w_dkv": w_dkv, "kv_lat_norm": kv_lat_norm, "w_ukv": w_ukv,
            "final_norm": final_norm}

def second_block(x, mem, positions, ffn1_norm, ffn1_w_gu, ffn1_w_down, mix_norm,
              ffn2_norm, ffn2_w_gu, ffn2_w_down, w_out, mem_norm, w_mem_kv,
              a_w_in, a_conv, a_A_log, a_dt_bias, a_out_norm,
              b_w_in, b_q_norm, b_w_uq, kv_in_norm, w_dkv, kv_lat_norm, w_ukv, final_norm):
    b, s, _ = x.shape
    mem_n = rms_norm(mem, mem_norm)
    cos, sin = rope_tables(positions, QK_ROPE)

    for i in range(N_A_LAYERS):
        l = i
        x = x + 0.5 * swiglu(rms_norm(x, ffn1_norm[l]), ffn1_w_gu[l], ffn1_w_down[l])
        h = rms_norm(x, mix_norm[l]) @ a_w_in[i]
        qkv, gate, b_raw, a_raw, q_mem = jnp.split(
            h, [3 * A_WIDTH, 4 * A_WIDTH, 4 * A_WIDTH + A_HEADS, 4 * A_WIDTH + 2 * A_HEADS], axis=-1)
        o_a = gated_deltanet(qkv, gate, b_raw, a_raw, a_conv[i], a_A_log[i], a_dt_bias[i], a_out_norm[i])
        o_m = memory_attention(q_mem, mem_n @ w_mem_kv[l])
        x = x + jnp.concatenate([o_a, o_m], axis=-1) @ w_out[l]
        x = x + 0.5 * swiglu(rms_norm(x, ffn2_norm[l]), ffn2_w_gu[l], ffn2_w_down[l])

    ckr = rms_norm(x, kv_in_norm) @ w_dkv
    c_kv = rms_norm(ckr[..., :KV_LORA], kv_lat_norm)
    k_rope = apply_rope(ckr[..., None, KV_LORA:], cos, sin)[:, :, 0]
    k_nope, v_mla = jnp.split((c_kv @ w_ukv).reshape(b, s, B_HEADS, QK_NOPE + V_HEAD), [QK_NOPE], axis=-1)

    for j in range(N_B_LAYERS):
        l = N_A_LAYERS + j
        x = x + 0.5 * swiglu(rms_norm(x, ffn1_norm[l]), ffn1_w_gu[l], ffn1_w_down[l])
        h = rms_norm(x, mix_norm[l]) @ b_w_in[j]
        cq, q_mem = jnp.split(h, [Q_LORA], axis=-1)
        q = (rms_norm(cq, b_q_norm[j]) @ b_w_uq[j]).reshape(b, s, B_HEADS, QK_NOPE + QK_ROPE)
        q_nope, q_rope = jnp.split(q, [QK_NOPE], axis=-1)
        q_rope = apply_rope(q_rope, cos, sin)
        o_b = mla_attention(q_nope, q_rope, k_nope, k_rope, v_mla)
        o_m = memory_attention(q_mem, mem_n @ w_mem_kv[l])
        x = x + jnp.concatenate([o_b, o_m], axis=-1) @ w_out[l]
        x = x + 0.5 * swiglu(rms_norm(x, ffn2_norm[l]), ffn2_w_gu[l], ffn2_w_down[l])

    return rms_norm(x, final_norm)


def setup_inputs(seed=0):
    out = dict(first_inputs(seed))
    for name, value in second_inputs(seed + 1).items():
        if name != "x":
            out[name + "_2"] = value
    return out


def reference(
    x, meta_tokens, norm_g, w_in, b_forget, pool_w, pool_scale, w_up_pool, w_up_attn, w_out,
    final_norm_g, mem_2, positions_2, ffn1_norm_2, ffn1_w_gu_2, ffn1_w_down_2, mix_norm_2,
    ffn2_norm_2, ffn2_w_gu_2, ffn2_w_down_2, w_out_2, mem_norm_2, w_mem_kv_2, a_w_in_2,
    a_conv_2, a_A_log_2, a_dt_bias_2, a_out_norm_2, b_w_in_2, b_q_norm_2, b_w_uq_2,
    kv_in_norm_2, w_dkv_2, kv_lat_norm_2, w_ukv_2, final_norm_2,
):
    x = first_block(
        x, meta_tokens, norm_g, w_in, b_forget, pool_w, pool_scale, w_up_pool, w_up_attn, w_out,
        final_norm_g,
    )
    return second_block(
        x, mem_2, positions_2, ffn1_norm_2, ffn1_w_gu_2, ffn1_w_down_2, mix_norm_2, ffn2_norm_2,
        ffn2_w_gu_2, ffn2_w_down_2, w_out_2, mem_norm_2, w_mem_kv_2, a_w_in_2, a_conv_2,
        a_A_log_2, a_dt_bias_2, a_out_norm_2, b_w_in_2, b_q_norm_2, b_w_uq_2, kv_in_norm_2,
        w_dkv_2, kv_lat_norm_2, w_ukv_2, final_norm_2,
    )


_drawn_inputs = setup_inputs


def setup_inputs(seed=0):
    import zlib

    import numpy as np

    out = dict(_drawn_inputs(seed))
    spreads = {}
    factors = {'norm_g': 4.756,
     'ffn1_norm_2': 4.481,
     'mix_norm_2': 3.507,
     'ffn2_norm_2': 5.605,
     'mem_norm_2': 8.0,
     'a_out_norm_2': 5.469,
     'b_q_norm_2': 8.0,
     'kv_in_norm_2': 8.0,
     'kv_lat_norm_2': 8.0,
     'final_norm_2': 2.814}
    for name, (base, spread) in spreads.items():
        noise = np.random.default_rng([zlib.crc32(name.encode()), seed]).standard_normal(out[name].shape)
        drawn = base * np.exp(spread * noise) if base else spread * noise
        out[name] = __import__('jax').numpy.asarray(drawn.astype(out[name].dtype))
    for name, factor in factors.items():
        out[name] = (out[name] * factor).astype(out[name].dtype)
    return out
```

```python
from contextlib import ExitStack

import numpy as np
import concourse.bass as bass
from concourse import mybir

F32 = mybir.dt.float32
F32R = mybir.dt.float32r
I32 = mybir.dt.int32
ALU = mybir.AluOpType
ACT = mybir.ActivationFunctionType
AX = mybir.AxisListType

P = 128
D = 1024
KC = D // P
SEQ = 256
META = 16
TOK = META + SEQ
FF = 2816
FT = FF // P
HD1 = 64
DH, DK = 6, 128
MEMH = 4
EPS = 1e-6
NEG = -1e30
TWO_PI = 2.0 * np.pi
_PART = round((TWO_PI - 6.28125) * 2 ** 20) / 2 ** 20
TWO_PI_PARTS = (6.28125, _PART, TWO_PI - 6.28125 - _PART)
ROUNDER = 1.5 * 2 ** 23
PI_DOWN = 3.141592502593994

STREAM = [
    ("w_in1", 20, 8), ("w_pool", 1, 2), ("w_up", 4, 8), ("w_out1", 4, 8), ("w_memkv", 4, 8),
    ("w_gu_a1", FT, 8), ("w_down_a1", 8, 11), ("w_in_a", 13, 8), ("w_out_a", 4, 8),
    ("w_gu_a2", FT, 8), ("w_down_a2", 8, 11),
    ("w_lat", 1, 8), ("w_krope", 1, 4), ("w_knope", 1, 6), ("w_vmla", 1, 6),
    ("w_gu_b1", FT, 8), ("w_down_b1", 8, 11), ("w_in_b", 2, 8), ("w_qnope", 1, 6),
    ("w_qrope", 1, 3), ("w_out_b", 4, 8), ("w_gu_b2", FT, 8), ("w_down_b2", 8, 11),
]
FIRST_SLAB, _s = {}, 0
for _name, _n, _b in STREAM:
    FIRST_SLAB[_name] = _s
    _s += _n
SLABS = _s
BLOCKS = [b for _, n, b in STREAM for _ in range(n)]
WHERE = [(name, i) for name, n, _ in STREAM for i in range(n)]
RAW = 4
RING = 4
UNIT = 11 * P


def first_unit(name):
    return 2 * FIRST_SLAB[name]


TILES = [
    ("forget", 1), ("in1", 39), ("pool", 4), ("up", 8), ("out1", 8), ("memkv", 8),
    ("gu_a1", 44), ("down_a1", 8), ("in_a", 18), ("ba", 1), ("in_a_tail", 8), ("vt", 3), ("delta", 18), ("kt", 2),
    ("out_a", 8), ("gu_a2", 44), ("down_a2", 8),
    ("lat", 2), ("krope", 1), ("krot", 1), ("knope", 6), ("vmla", 4),
    ("gu_b1", 44), ("down_b1", 8), ("in_b", 4), ("qnope", 6), ("qrope", 3), ("qrot", 3),
    ("out_b", 8), ("gu_b2", 44), ("down_b2", 8),
]
FIRST_TILE, _t = {}, 0
for _name, _n in TILES:
    FIRST_TILE[_name] = _t
    _t += _n

NORMS = [("in1", 8), ("mem", 8), ("end1", 8), ("ffn_a1", 8), ("mix_a", 8), ("ffn_a2", 8),
         ("kv", 8), ("kvlat", 2), ("mix_b", 8), ("qlat", 2), ("ffn_b2", 8), ("end2", 8)]
NORM = {name: n for n, (name, _) in enumerate(NORMS)}
SQ0 = {name: sum(c for _, c in NORMS[:n]) for n, (name, _) in enumerate(NORMS)}
SPLITS = ["in1", "mem", "ffn_a1", "mix_a", "ffn_a2", "kv", "ffn_b1", "mix_b", "ffn_b2"]
XG0 = {name: 8 * n for n, name in enumerate(SPLITS)}

GAINS = ["in1", "end1", "mem", "ffn_a1", "mix_a", "ffn_a2", "kv", "ffn_b1", "mix_b", "ffn_b2", "end2"]
GAIN = {name: 8 * n for n, name in enumerate(GAINS)}
C_POOL = 8 * len(GAINS)
C_CONV = C_POOL + 4
C_OUTG = C_CONV + 72
C_QLAT = C_OUTG + 1
C_KVLAT = C_QLAT + 2
C_BF = C_KVLAT + 2
C_DT = C_BF + 1
C_ALOG = C_DT + 1
C_INV = C_ALOG + 1
N_PARAM = C_INV + 1

K_ID = 0
K_ONE = K_ID + P
K_ROT = K_ONE + P
K_MASK1 = K_ROT + P
N_MASK1 = 144 + 272
K_MASK2 = K_MASK1 + N_MASK1
N_MASK2 = 128 + 256
K_LEV = K_MASK2 + N_MASK2
K_CAUS = K_LEV + 7 * P
N_CONST = K_CAUS + P

MEM_A, MEM_B, MLA = 8, 12, 16
FFNS = ["a1", "a2", "b1", "b2"]
FFN_NORM = {"a1": "ffn_a1", "a2": "ffn_a2", "b1": "ffn_b1", "b2": "ffn_b2"}
FFN_THEN = {"a1": "mix_a", "a2": "kv", "b1": "mix_b", "b2": "end2"}


SCALE = {"forget": HD1 ** -0.5, "mem_a": 64 ** -0.5, "mem_b": 64 ** -0.5, "mla": (128 + 64) ** -0.5}


def kind(a):
    return "forget" if a < MEM_A else "mem_a" if a < MEM_B else "mem_b" if a < MLA else "mla"


def copies_before(a):
    return 2 * min(a, MEM_A) + max(a - MEM_A, 0)


def outputs_before(a):
    return min(a, MLA) // 2 + max(a - MLA, 0)


def program(nc, dram, out):
    with ExitStack() as ctx:
        def place(name, at, shape, dtype=F32):
            return (nc.alloc_sbuf_tensor_at(name, list(shape), dtype, offset=at),
                    (at + int(np.prod(shape[1:])) * 4 + 31) // 32 * 32)

        x, at = place("x", (nc.sbuf_base + 31) // 32 * 32, [P, KC, SEQ])
        xg_hi, at = place("xg_hi", at, [P, KC, TOK], F32R)
        xg_lo, at = place("xg_lo", at, [P, KC, TOK], F32R)
        raw, at = place("raw", at, [P, RAW, 2, UNIT])
        w_hi, at = place("w_hi", at, [P, RING, UNIT], F32R)
        w_lo, at = place("w_lo", at, [P, RING, UNIT], F32R)
        acc, at = place("acc", at, [P, TOK])
        sq, at = place("sq", at, [P, 2, TOK])
        root, at = place("root", at, [P, TOK])
        rstd, at = place("rstd", at, [P, TOK])
        rstd_mem, at = place("rstd_mem", at, [P, SEQ])
        par, at = place("par", at, [P, N_PARAM])
        const, at = place("const", at, [P, N_CONST])
        mem_k, at = place("mem_k", at, [P, 2, 2, SEQ])
        mem_v, at = place("mem_v", at, [P, 2, 2, SEQ])
        cos, at = place("cos", at, [P, SEQ])
        sin, at = place("sin", at, [P, SEQ])
        small, at = place("small", at, [P, 96])
        ident_r, at = place("ident_r", at, [24, 24], F32R)
        free0 = at

        h_hi, at = place("h_hi", free0, [P, FT, SEQ], F32R)
        h_lo, at = place("h_lo", at, [P, FT, SEQ], F32R)
        mix_end = at
        gate_n, at = place("gate_n", at, [P, 2, SEQ])
        gate_s, at = place("gate_s", at, [P, 2, SEQ])
        hid, at = place("hid", at, [P, 2, SEQ])
        k_nope, at = place("k_nope", at, [P, 6, SEQ])
        k_rope, at = place("k_rope", at, [P, SEQ])
        v_mla, at = place("v_mla", at, [P, 2, 6 * P])
        assert at <= nc.sbuf_usable_end

        q1, at = place("q1", free0, [P, 4, SEQ])
        k1, at_v = place("k1", at, [P, 4, TOK])
        v1, at = place("v1", at_v, [P, 3, 512])
        s1, at = place("s1", at, [P, 2, N_MASK1])
        pt1, at_z = place("pt1", at, [P, 640])
        z_attn, at = place("z_attn", at_z, [P, 4, SEQ])
        z_pool, at_u = place("z_pool", at, [P, 4, SEQ])
        u1, at = place("u1", at_u, [P, 4, TOK])
        pooled, at_g = place("pooled", at, [P, 4, SEQ])
        gates, at_o = place("gates", at_g, [P, KC, 2, SEQ])
        o1, at_m = place("o1", at_o, [P, 4, SEQ])
        mem_x, at = place("mem_x", at_m, [P, KC, SEQ])
        y1, at = place("y1", at, [P, 4, SEQ])
        assert at <= nc.sbuf_usable_end
        x0, at = place("x0", at_g, [P, KC, TOK])
        wf, at = place("wf", at, [P, 184])
        wf_hi, at = place("wf_hi", at, [P, 184], F32R)
        wf_lo, at = place("wf_lo", at, [P, 184], F32R)
        pos, at = place("pos", at_o, [P, SEQ], I32)
        ang, at = place("ang", at, [P, SEQ])
        turn, at = place("turn", at, [P, SEQ])
        lf, at = place("lf", at_m, [8, SEQ + META])
        lf2, at = place("lf2", at, [8, SEQ + META])
        pool_tmp, at = place("pool_tmp", at, [P, 2, TOK])
        c8, at = place("c8", at, [8, TOK])
        pool_hi, at = place("pool_hi", free0, [P, 4, SEQ], F32R)
        pool_lo, at = place("pool_lo", at, [P, 4, SEQ], F32R)
        y_hi, at = place("y_hi", at_u, [P, 8, SEQ], F32R)
        y_lo, at = place("y_lo", at_v, [P, 8, SEQ], F32R)
        mem_hi, at = place("mem_hi", at_g, [P, KC, SEQ], F32R)
        mem_lo, at = place("mem_lo", at, [P, KC, SEQ], F32R)
        gated, at = place("gated", at_o, [P, 2, 512])
        merged, at = place("merged", at_m + 8192, [P, 2, SEQ])

        kqv, at = place("kqv", free0, [P, 18, SEQ])
        gate_a, at = place("gate_a", at, [P, DH, SEQ])
        qm_a, at_w = place("qm_a", at, [P, 2, SEQ])
        cx, at = place("cx", at_w, [P, 2, SEQ + 4])
        cy, at = place("cy", at, [P, 2, SEQ])
        csq, at = place("csq", at, [P, 2, SEQ])
        dec, at = place("dec", at_w, [P, 2, 4, SEQ])
        inv_x, at = place("inv_x", at_w, [P, 2, 512])
        inv_c, at = place("inv_c", at, [P, 2, 512])
        rhs1, at = place("rhs1", at_w, [P, DH, P])
        vn1, at = place("vn1", at, [P, DH, P])
        ba, at = place("ba", at_w + 8192, [38, SEQ])
        rows_hi, at = place("rows_hi", at, [24, SEQ], F32R)
        cols, at = place("cols", at, [P, 256])
        rows_lo, _ = place("rows_lo", at, [24, SEQ], F32R)
        sp1, at = place("sp1", at, [38, SEQ])
        sp2, at = place("sp2", at, [38, SEQ])
        n_t, at_a = place("n_t", at, [P, 12, P])
        a_t, at_d = place("a_t", at_a, [P, 12, P])
        d_lo, at_dt = place("d_lo", at_d, [P, 12, P])
        d_t, at_k = place("d_t", at_dt, [P, 12, P])
        k_dec, at = place("k_dec", at_k, [P, DH, P])
        osq = [k_dec, rhs1]
        om_a, at = place("om_a", at, [P, 2, SEQ])
        assert at <= nc.sbuf_usable_end
        wba, at = place("wba", at_a, [P, 394])
        wba_hi, at = place("wba_hi", at, [P, 394], F32R)
        wba_lo, at = place("wba_lo", at, [P, 394], F32R)
        o_a, at = place("o_a", at_d, [P, DH, SEQ])
        state, at = place("state", at_a - 6144, [P, DH, P])
        vn0, at = place("vn0", at, [P, DH, P])
        p_a, at = place("p_a", at_dt, [P, 2, 512])
        pt_a, at = place("pt_a", at, [P, 512])
        cat_hi_a, at = place("cat_hi_a", free0, [P, 8, SEQ], F32R)
        cat_lo_a, at = place("cat_lo_a", at, [P, 8, SEQ], F32R)

        lat, at = place("lat", free0, [P, 2, SEQ])
        lat_hi, at = place("lat_hi", at, [P, 2, SEQ], F32R)
        lat_lo, at = place("lat_lo", at, [P, 2, SEQ], F32R)
        rot_s, at = place("rot_s", at, [P, SEQ])
        s_b, at = place("s_b", at + 1024, [P, 2, 512])
        pt_b, at = place("pt_b", at, [P, 512])
        o_b, at = place("o_b", at, [P, 8, SEQ])
        qm_b, at = place("qm_b", at, [P, 2, SEQ])
        q_nope, at_c = place("q_nope", at, [P, 6, SEQ])
        q_rope, at = place("q_rope", at_c, [P, 3, SEQ])
        cat_hi_b, at = place("cat_hi_b", at, [P, 8, SEQ], F32R)
        assert at <= mix_end
        cat_lo_b, at = place("cat_lo_b", free0, [P, 8, SEQ], F32R)

        eps_c, one_c = small[:, 0:1], small[:, 1:2]
        rc1, rcm = small[:, 4:7], small[:, 8:10]
        row_max, neg_max = small[:, 12:16], small[:, 16:20]
        row_sum, row_inv = small[:, 20:24], small[:, 24:28]

        ba_col = cols[:, 0:76].rearrange("p (c r) -> p c r", c=2)
        b_col, g_col = ba_col[:, :, 0:6], ba_col[:, :, 32:38]
        kq_inv = cols[:, 80:104].rearrange("p (c h) -> p c h", c=2)
        packed = cols[:, 104:152].rearrange("p (c h) -> p c h", c=2)
        e_g = cols[:, 152:164].rearrange("p (c h) -> p c h", c=2)
        k_neg = cols[:, 164:176].rearrange("p (c h) -> p c h", c=2)
        g_last = cols[:, 176:182]
        kq_root = cols[:, 184:208].rearrange("p (c h) -> p c h", c=2)
        o_root, o_inv = cols[:, 208:220], cols[:, 220:232]
        k_scale = cols[:, 232:238]

        main = [ctx.enter_context(nc.psum_tensor(f"main{i}", [P, 512], F32)) for i in range(4)]
        side = [ctx.enter_context(nc.psum_tensor(f"side{i}", [P, 512], F32)) for i in range(4)]

        def sem(name):
            return ctx.enter_context(nc.semaphore(name))

        landed = [sem(f"landed{r}") for r in range(RAW)]
        hi_ready, lo_ready = sem("hi_ready"), sem("lo_ready")
        unit_used = sem("unit_used")
        evac = sem("evac")
        par_in, x_in, mem_in, pos_in, wf_in, wba_in, const_in, mask_in = (
            sem(n) for n in ("par_in", "x_in", "mem_in", "pos_in", "wf_in", "wba_in", "const_in", "mask_in"))
        x0_in = [sem("x0_in0"), sem("x0_in1")]
        sq_ready, acc_clear, acc_done = sem("sq_ready"), sem("acc_clear"), sem("acc_done")
        xh_ready, xg_ready = sem("xh_ready"), sem("xg_ready")
        ss_ready, root_ready, rstd_ready = sem("ss_ready"), sem("root_ready"), sem("rstd_ready")
        dve_chain, act_chain, pool_chain = sem("dve_chain"), sem("act_chain"), sem("pool_chain")
        consts_set, ident_ready = sem("consts_set"), sem("ident_ready")
        small_hi, small_lo, extra_done = sem("small_hi"), sem("small_lo"), sem("extra_done")
        col_ready, col_copied = sem("col_ready"), sem("col_copied")
        f_ready, f_act, c_ready = sem("f_ready"), sem("f_act"), sem("c_ready")
        scores_ready, rowmax_ready, exp_ready = sem("scores_ready"), sem("rowmax_ready"), sem("exp_ready")
        probs_ready, pt_ready, pt_copied = sem("probs_ready"), sem("pt_ready"), sem("pt_copied")
        heads_done, o_copied = sem("heads_done"), sem("o_copied")
        pooled_ready, pool_hi_ready, pool_split = sem("pooled_ready"), sem("pool_hi_ready"), sem("pool_split")
        act_z, y_done, y_hi_ready, y_split = sem("act_z"), sem("y_done"), sem("y_hi_ready"), sem("y_split")
        sum_done, merged_hi, merged_split = sem("sum_done"), sem("merged_hi"), sem("merged_split")
        x_new = sem("x_new")
        ang_ready, trig = sem("ang_ready"), sem("trig")
        silu_ready, hid_ready, h_hi_ready, h_ready = (
            sem("silu_ready"), sem("hid_ready"), sem("h_hi_ready"), sem("h_ready"))
        conv0, conv_done, csilu, csq_ready, csum = (
            sem("conv0"), sem("conv_done"), sem("csilu"), sem("csq_ready"), sem("csum"))
        gate_silu, tap_done = sem("gate_silu"), sem("tap_done")
        ba_act, ba_dve, ba_t, col_act, cpk_ready, rows_t, rows_ready = (
            sem(n) for n in ("ba_act", "ba_dve", "ba_t", "col_act", "cpk_ready", "rows_t", "rows_ready"))
        spread, gram, diff_ready, decay_ready, n_ready = (
            sem(n) for n in ("spread", "gram", "diff_ready", "decay_ready", "n_ready"))
        turned_v, turned_k = sem("turned_v"), sem("turned_k")
        c_masked, x_ready, x_copied, dx_ready, d_dve, turned, turn_copied = (
            sem(n) for n in ("c_masked", "x_ready", "x_copied", "dx_ready", "d_dve", "turned", "turn_copied"))
        rec_pe, rec_act, rec_dve = sem("rec_pe"), sem("rec_act"), sem("rec_dve")
        og_pe, og_act, og_dve = sem("og_pe"), sem("og_act"), sem("og_dve")
        cat_hi_ready, cat_ready = sem("cat_hi_ready"), sem("cat_ready")
        lat_done, lat_hi_ready, lat_ready = sem("lat_done"), sem("lat_hi_ready"), sem("lat_ready")
        rope_ready = sem("rope_ready")
        out_ready, stored = sem("out_ready"), sem("stored")

        ident = const[:, K_ID:K_ID + P]
        ones = const[:, K_ONE:K_ONE + P]
        rot = const[:, K_ROT:K_ROT + P]

        def gain(name, m):
            return par[:, GAIN[name] + m:GAIN[name] + m + 1] if isinstance(m, int) else \
                par[:, bass.ds(m + GAIN[name], 1)]

        def piece(tensor, u, b, n=1):
            return tensor[:, u % RING, b * P:(b + n) * P]

        def score_parts(a):
            if kind(a) == "forget":
                return s1[:, a % 2, :], (0, 144), (144, 272)
            if kind(a) == "mla":
                return s_b[:, a % 2, :], (0, 128), (128, 256)
            return (p_a if kind(a) == "mem_a" else s_b)[:, a % 2, :], (0, 256), (256, 256)

        def key_blocks(a):
            if kind(a) == "forget":
                return [(META, P, 0, side[1], 0, 0), (META + P, P, 1, side[1], 256, 256),
                        (0, META, 0, side[3], 0, 384)]
            second = 1 if kind(a) == "mla" else 0
            return [(0, P, 0, side[1], 0, 0), (P, P, second, side[1], 256, 256)]

        def probs_t(a):
            return {"forget": pt1, "mem_a": pt_a}.get(kind(a), pt_b)

        def chunks_of(j):
            return [0, 1] if j == 0 else [j + 1] if j < KC - 1 else []

        def scale_bank(j):
            return main[(FIRST_TILE["out_a"] + 1 + j) % 4]

        def score_bank(a):
            return side[3] if a >= MEM_B and a % 2 else side[0]

        block = ctx.enter_context(nc.Block())

        @block.sync
        def _(sp):
            def load(s, off=0, step=None):
                name, i = WHERE[s]
                if s >= RAW:
                    sp.wait_ge(lo_ready, 2 * (s - RAW + 1) + off)
                src = dram[name][i] if step is None else dram[name][step + i]
                sp.dma_start(raw[:, s % RAW, :, 0:BLOCKS[s] * P], src).then_inc(landed[s % RAW], 16)

            def load_all(name, n, first=0):
                s0 = FIRST_SLAB[name] + first
                turns = (n - first) // RAW if n - first >= 2 * RAW else 0
                if turns:
                    with sp.Fori(0, turns) as i:
                        for j in range(RAW):
                            load(s0 + j, i * (2 * RAW), i * RAW)
                for j in range(turns * RAW, n - first):
                    load(s0 + j)

            for j in range(2):
                half = slice(KC // 2 * j, KC // 2 * (j + 1))
                sp.dma_start(x0[:, half, :], dram["x0"][:, half, :]).then_inc(x0_in[j], 16)
            for j in range(RAW):
                load(j)
            sp.dma_start(x[:, :, :], dram["x"]).then_inc(x_in, 16)
            for name, n, _ in STREAM:
                load_all(name, n, RAW if name == "w_in1" else 0)
            for m in range(KC):
                sp.wait_ge(out_ready, m + 1)
                sp.dma_start(out[m], x[:, m, :]).then_inc(stored, 16)
            sp.wait_ge(stored, 16 * KC)

        @block.scalar
        def _(act):
            local = [0]

            def link(ins):
                local[0] += 1
                ins.then_inc(act_chain, 1)
                act.wait_ge(act_chain, local[0])

            def split_hi(u, off=0):
                s = u // 2
                n = BLOCKS[s] * P
                if u % 2 == 0:
                    act.wait_ge(landed[s % RAW], 16 * (s // RAW + 1) + off * 2)
                if u >= RING:
                    act.wait_ge(unit_used, u - RING + 1 + off)
                act.activation(w_hi[:, u % RING, 0:n], raw[:, s % RAW, u % 2, 0:n],
                               ACT.Copy).then_inc(hi_ready, 1)

            def slot(u, off=0):
                if u + RING < 2 * SLABS:
                    split_hi(u + RING, off)

            def square_free(c, off=0):
                if c >= 2:
                    act.wait_ge(acc_done, c - 1 + off)

            def square(src, n, c):
                act.activation(sq[:, c % 2, 0:n], src, ACT.Square).then_inc(sq_ready, 1)

            def scale_hi(dst, src, g):
                act.activation(dst, src, ACT.Copy, scale=g).then_inc(xh_ready, 1)

            def root_of(name, n, width=D):
                act.wait_ge(ss_ready, NORM[name] + 1)
                if NORM[name] > 0:
                    act.wait_ge(rstd_ready, NORM[name])
                act.activation(root[:, 0:n], side[3][:, 0:n], ACT.Sqrt, bias=eps_c,
                               scale=1.0 / width).then_inc(root_ready, 1)

            def exps(a):
                buf, *parts = score_parts(a)
                src = score_bank(a) if kind(a).startswith("mem") else buf
                act.wait_ge(rowmax_ready, a + 1)
                if a >= 2:
                    act.wait_ge(pt_ready, a - 1)
                for t, (c, n) in enumerate(parts):
                    i = 2 * (a % 2) + t
                    act.activation(buf[:, c:c + n], src[:, c:c + n], ACT.Exp, bias=neg_max[:, i:i + 1],
                                   scale=SCALE[kind(a)], accum_out=row_sum[:, i:i + 1]).then_inc(exp_ready, 1)

            def copy_pt(a):
                act.wait_ge(pt_ready, a + 1)
                if a > 0:
                    act.wait_ge(heads_done, a)
                n = 512 if kind(a).startswith("mem") else 384
                act.activation(probs_t(a)[:, 0:n], side[1][:, 0:n], ACT.Copy).then_inc(pt_copied, 1)
                if kind(a) == "forget":
                    act.activation(pt1[0:META, 384:640], side[3][0:META, 0:256], ACT.Copy)\
                       .then_inc(pt_copied, 1)

            act.dma_start(par[:, :], dram["par"]).then_inc(par_in, 16)
            act.dma_start(wf[:, :], dram["w_forget"]).then_inc(wf_in, 16)
            act.dma_start(const[:, 0:K_ROT], dram["const"][:, 0:K_ROT]).then_inc(const_in, 16)
            act.dma_start(pos[:, :], dram["pos"]).then_inc(pos_in, 16)
            act.dma_start(const[:, K_ROT:], dram["const"][:, K_ROT:]).then_inc(mask_in, 16)

            act.wait_ge(par_in, 16)
            for k in range(KC):
                act.wait_ge(x0_in[k // (KC // 2)], 16)
                square_free(k)
                scale_hi(xg_hi[:, k, :], x0[:, k, :], gain("in1", k))
                square(x0[:, k, :], TOK, k)
                if k == 0:
                    act.wait_ge(wf_in, 16)
                    act.activation(wf_hi[:, :], wf[:, :], ACT.Copy).then_inc(small_hi, 1)
            for u in range(RING):
                if u == 2:
                    act.wait_ge(consts_set, 2)
                    root_of("in1", TOK)
                split_hi(u)

            t0 = FIRST_TILE["in1"]
            for u in range(40):
                a = u - 12
                if 0 <= a < MEM_A:
                    exps(a)
                slot(u)
                if 0 <= a - 1 < MEM_A:
                    copy_pt(a - 1)
                if u == 2:
                    act.wait_ge(f_ready, 1)
                    link(act.activation(lf2[:, :], lf[:, :], ACT.Abs))
                    link(act.activation(lf2[:, :], lf2[:, :], ACT.Exp, scale=-1.0))
                    act.activation(lf2[:, :], lf2[:, :], ACT.Ln, bias=one_c[0:8, :]).then_inc(f_act, 1)
                    act.wait_ge(const_in, 16)
                    act.activation(ident_r[:, :], ident[0:24, 0:24], ACT.Copy).then_inc(ident_ready, 1)
                if u == 7:
                    act.wait_ge(ang_ready, 1)
                    act.activation(cos[:, :], ang[:, :], ACT.Sin).then_inc(trig, 1)
                    act.wait_ge(ang_ready, 2)
                    act.activation(sin[:, :], turn[:, :], ACT.Sin).then_inc(trig, 1)
                if u == 22:
                    act.wait_ge(pooled_ready, 4)
                    act.wait_ge(scores_ready, 8)
                    act.activation(pool_hi[:, :, :], pooled[:, :, :], ACT.Copy).then_inc(pool_hi_ready, 1)
                    act.dma_start(mem_x[:, :, :], dram["mem"]).then_inc(mem_in, 16)
                if u == 24:
                    act.wait_ge(evac, t0 + 15)
                    act.activation(z_attn[:, :, :], z_attn[:, :, :], ACT.Silu).then_inc(act_z, 1)
                if u == 25:
                    act.wait_ge(evac, t0 + 23)
                    act.activation(z_pool[:, :, :], z_pool[:, :, :], ACT.Silu).then_inc(act_z, 1)
                if u == 27:
                    act.wait_ge(y_done, 1)
                    act.activation(y_hi[:, 4:8, :], y1[:, :, :], ACT.Copy).then_inc(y_hi_ready, 1)
                if 28 <= u < 36:
                    if u == 28:
                        act.wait_ge(mem_in, 16)
                    square_free(SQ0["mem"] + u - 28)
                    square(mem_x[:, u - 28, :], SEQ, SQ0["mem"] + u - 28)
                if u == 33:
                    act.wait_ge(evac, t0 + 31)
                    act.activation(gates[:, :, 0, :], gates[:, :, 0, :], ACT.Sigmoid).then_inc(act_z, 1)

            act.wait_ge(evac, FIRST_TILE["pool"] + 4)
            act.activation(y_hi[:, 0:4, :], y1[:, :, :], ACT.Copy).then_inc(y_hi_ready, 1)
            for j in range(2):
                slot(first_unit("w_pool") + j)
            act.wait_ge(evac, t0 + 39)
            act.activation(gates[:, :, 1, :], gates[:, :, 1, :], ACT.Sigmoid).then_inc(act_z, 1)
            root_of("mem", SEQ)
            for m in range(KC):
                act.wait_ge(sum_done, m + 1)
                act.activation(xg_hi[:, m, 0:SEQ], merged[:, m % 2, :], ACT.Copy).then_inc(merged_hi, 1)
                slot(first_unit("w_up") + m)
            for m in range(KC):
                scale_hi(mem_hi[:, m, :], mem_x[:, m, :], gain("mem", m))
                act.wait_ge(evac, FIRST_TILE["out1"] + m + 1)
                square_free(SQ0["end1"] + m)
                square(x[:, m, :], SEQ, SQ0["end1"] + m)
                slot(first_unit("w_out1") + m)
            root_of("end1", SEQ)
            for j in range(KC):
                for k in chunks_of(j):
                    act.wait_ge(x_new, k + 1)
                    scale_hi(xg_hi[:, k, 0:SEQ], x[:, k, :], gain("ffn_a1", k))
                    square_free(SQ0["ffn_a1"] + k)
                    square(x[:, k, :], SEQ, SQ0["ffn_a1"] + k)
                slot(first_unit("w_memkv") + j)

            def residual(m, t, c, name, i, per):
                act.wait_ge(evac, t + m + 1 + i * per)
                row = m if isinstance(i, int) else i * per + m
                square_free(c + m, i * per)
                if name != "end2":
                    scale_hi(xg_hi[:, row, 0:SEQ], x[:, row, :], gain(name, row))
                square(x[:, row, :], SEQ, c + m)

            def ffn(which):
                f, u0, t0 = FFNS.index(which), first_unit("w_gu_" + which), FIRST_TILE["gu_" + which]
                then = FFN_THEN[which]
                if which != "b1":
                    root_of(FFN_NORM[which], SEQ)

                def up(t, i=0):
                    slot(u0 + 2 * t, i * 8)
                    act.wait_ge(evac, t0 + 2 * t + 1 + i * 8)
                    act.activation(gate_s[:, t % 2, :], gate_n[:, t % 2, :], ACT.Silu).then_inc(silu_ready, 1)
                    slot(u0 + 2 * t + 1, i * 8)
                    row = t if isinstance(i, int) else i * 4 + t
                    act.wait_ge(hid_ready, f * FT + t + 1 + i * 4)
                    act.activation(h_hi[:, row, :], hid[:, t % 2, :], ACT.Copy).then_inc(h_hi_ready, 1)

                with act.Fori(0, FT // 4) as i:
                    for t in range(4):
                        up(t, i)
                for t in range(FT // 4 * 4, FT):
                    up(t)
                last = which == "b2"
                u0 = first_unit("w_down_" + which)
                if not last:
                    with act.Fori(0, 2) as i:
                        for m in range(4):
                            slot(u0 + 2 * m, i * 8)
                            residual(m, FIRST_TILE["down_" + which], SQ0[then], then, i, 4)
                            slot(u0 + 2 * m + 1, i * 8)
                else:
                    for m in range(KC):
                        slot(u0 + 2 * m)
                        residual(m, FIRST_TILE["down_" + which], SQ0[then], then, 0, 0)
                        slot(u0 + 2 * m + 1)

            def mix_out(name, then):
                for m in range(KC):
                    residual(m, FIRST_TILE[name], SQ0[then], then, 0, 0)
                    slot(first_unit("w_" + name) + m)

            ffn("a1")

            u0, t0 = first_unit("w_in_a"), FIRST_TILE["in_a"]
            root_of("mix_a", SEQ)
            act.dma_start(wba[:, :], dram["w_ba"]).then_inc(wba_in, 16)
            for t in range(26):
                h = t - 21
                if 0 <= h < MEMH:
                    exps(MEM_A + h)
                slot(u0 + t)
                if t < 18:
                    if t >= 2:
                        act.wait_ge(csilu, t - 1)
                    act.wait_ge(evac, t0 + t + 1)
                    act.activation(cy[:, t % 2, :], cx[:, t % 2, 3:3 + SEQ], ACT.Copy,
                                   scale=par[:, C_CONV + 4 * t + 3:C_CONV + 4 * t + 4]).then_inc(conv0, 1)
                if 1 <= t <= 18:
                    act.wait_ge(conv_done, t)
                    act.activation(kqv[:, t - 1, :], cy[:, (t - 1) % 2, :], ACT.Silu).then_inc(csilu, 1)
                if 1 <= t <= 12:
                    act.wait_ge(csilu, t)
                    if t > 2:
                        act.wait_ge(csum, t - 2)
                    act.activation(csq[:, (t - 1) % 2, :], kqv[:, t - 1, :], ACT.Square).then_inc(csq_ready, 1)
                if t == 10:
                    act.wait_ge(wba_in, 16)
                    act.activation(wba_hi[:, :], wba[:, :], ACT.Copy).then_inc(small_hi, 1)
                if t == 18:
                    act.wait_ge(csum, 12)
                    act.activation(kq_root, side[3][:, 0:24].rearrange("p (c h) -> p c h", c=2), ACT.Sqrt,
                                   bias=eps_c).then_inc(col_act, 1)
                if t == 19:
                    act.wait_ge(evac, FIRST_TILE["ba"] + 1)
                    act.activation(ba[0:6, :], ba[0:6, :], ACT.Sigmoid).then_inc(ba_act, 1)
                    act.wait_ge(ba_dve, 1)
                    link(act.activation(sp2[32:38, :], sp1[32:38, :], ACT.Abs))
                if t == 20:
                    act.activation(small[32:38, 30:31], par[32:38, C_ALOG:C_ALOG + 1], ACT.Exp).then_inc(ba_act, 1)
                    link(act.activation(sp2[32:38, :], sp2[32:38, :], ACT.Exp, scale=-1.0))
                if t == 21:
                    act.activation(sp2[32:38, :], sp2[32:38, :], ACT.Ln, bias=one_c[32:38, :]).then_inc(ba_act, 1)
                if 0 <= h - 1 < MEMH:
                    copy_pt(MEM_A + h - 1)
            act.wait_ge(col_copied, 3)
            act.activation(e_g, g_col, ACT.Exp).then_inc(col_act, 1)
            for h in range(DH):
                act.wait_ge(diff_ready, 3 * h + 3)
                act.activation(dec[:, h % 2, 1, :], dec[:, h % 2, 0, :], ACT.Exp).then_inc(decay_ready, 1)
            act.activation(g_last, g_last, ACT.Exp).then_inc(col_act, 1)
            for s in range(23):
                if s < 3:
                    act.wait_ge(turned, s + 1)
                    act.activation(d_lo[:, 4 * s:4 * s + 4, :], side[s % 2][:, :], ACT.Copy).then_inc(turn_copied, 1)
                if s in (8, 11, 14):
                    pair = slice(2 * (s - 8) // 3, 2 * (s - 8) // 3 + 2)
                    act.wait_ge(evac, FIRST_TILE["in_a_tail"] + 8)
                    act.activation(gate_a[:, pair, :], gate_a[:, pair, :], ACT.Silu).then_inc(gate_silu, 1)
                if 3 <= s < 21:
                    n = s - 3
                    act.wait_ge(x_ready, n + 1)
                    if n >= 2:
                        act.wait_ge(dx_ready, n - 1)
                    act.activation(inv_x[:, n % 2, :], main[n % 2][:, :], ACT.Copy).then_inc(x_copied, 1)
                if 3 <= s - 2 < 18:
                    n = s - 2
                    act.wait_ge(turned, n + 1)
                    g = n % 3
                    act.activation(d_t[:, 4 * g:4 * g + 4, :], side[n % 2][:, :], ACT.Copy).then_inc(turn_copied, 1)
            for n, (dst, bank, heads, seen) in enumerate((
                    (vn0, main[0], (0, 4), 1), (vn0, main[1], (4, 6), 2),
                    (vn1, main[2], (0, 4), 9), (vn1, main[3], (4, 6), 10))):
                if n == 2:
                    act.wait_ge(rec_dve, 4)
                    act.activation(osq[0][:, :, :], o_a[:, :, 0:P], ACT.Square).then_inc(og_act, 1)
                act.wait_ge(rec_pe, seen)
                a, b = heads
                act.activation(dst[:, a:b, :], bank[:, 0:(b - a) * P], ACT.Copy).then_inc(rec_act, 1)
            act.wait_ge(rec_dve, 12)
            act.activation(osq[1][:, :, :], o_a[:, :, P:SEQ], ACT.Square).then_inc(og_act, 1)
            act.wait_ge(og_pe, 1)
            act.activation(o_root, side[3][:, 0:12], ACT.Sqrt, bias=eps_c, scale=1.0 / DK).then_inc(og_act, 1)
            act.wait_ge(o_copied, outputs_before(MEM_B))
            act.activation(cat_hi_a[:, 6:8, :], om_a[:, :, :], ACT.Copy).then_inc(cat_hi_ready, 1)
            for j in range(3):
                act.wait_ge(og_dve, 2 + 2 * (j + 1))
                act.activation(cat_hi_a[:, 2 * j:2 * j + 2, :], o_a[:, 2 * j:2 * j + 2, :], ACT.Copy)\
                   .then_inc(cat_hi_ready, 1)
            mix_out("out_a", "ffn_a2")
            ffn("a2")

            root_of("kv", SEQ)
            for j in range(2):
                act.wait_ge(evac, FIRST_TILE["lat"] + j + 1)
                square_free(SQ0["kvlat"] + j)
                square(lat[:, j, :], SEQ, SQ0["kvlat"] + j)
                slot(first_unit("w_lat") + j)
            for j in range(2):
                slot(first_unit("w_krope") + j)
            root_of("kvlat", SEQ, 256)
            act.wait_ge(lat_done, 2)
            act.activation(lat_hi[:, :, :], lat[:, :, :], ACT.Copy).then_inc(lat_hi_ready, 1)
            act.wait_ge(unit_used, first_unit("w_knope"))
            for k in range(KC):
                scale_hi(xg_hi[:, k, 0:SEQ], x[:, k, :], gain("ffn_b1", k))
                if k in (1, 3, 5, 7):
                    slot(first_unit("w_knope") + k // 2)
            ffn("b1")

            root_of("mix_b", SEQ)
            for j in range(4):
                slot(first_unit("w_in_b") + j)
                if j < 2:
                    act.wait_ge(evac, FIRST_TILE["in_b"] + j + 1)
                    square_free(SQ0["qlat"] + j)
                    square(lat[:, j, :], SEQ, SQ0["qlat"] + j)
            root_of("qlat", SEQ, 256)
            for i in range(MEMH + 2):
                if i < MEMH:
                    exps(MEM_B + i)
                if i == 0:
                    act.wait_ge(lat_done, 4)
                    act.activation(lat_hi[:, :, :], lat[:, :, :], ACT.Copy).then_inc(lat_hi_ready, 1)
                if 1 <= i <= 4:
                    slot(first_unit("w_qnope") + i - 1)
                if i >= 2:
                    copy_pt(MEM_B + i - 2)
            for i in range(DH + 4):
                if i < DH:
                    exps(MLA + i)
                if 0 <= i - 2 < DH:
                    copy_pt(MLA + i - 2)
                if i == 0:
                    act.wait_ge(o_copied, outputs_before(MLA))
                    act.activation(cat_hi_b[:, 6:8, :], o_b[:, 6:8, :], ACT.Copy).then_inc(cat_hi_ready, 1)
                if i >= 4:
                    act.wait_ge(o_copied, outputs_before(MLA + i - 3))
                    act.activation(cat_hi_b[:, i - 4, :], o_b[:, i - 4, :], ACT.Copy).then_inc(cat_hi_ready, 1)
            mix_out("out_b", "ffn_b2")
            ffn("b2")
            root_of("end2", SEQ)

        @block.vector
        def _(dve):
            local = [0]

            def link(ins):
                local[0] += 1
                ins.then_inc(dve_chain, 1)
                dve.wait_ge(dve_chain, local[0])

            def low(dst, src, hi):
                return dve.tensor_tensor(dst, src, hi.bitcast(F32), ALU.subtract)

            def split_lo(u, off=0):
                s = u // 2
                n = BLOCKS[s] * P
                dve.wait_ge(hi_ready, u + 1 + off)
                low(w_lo[:, u % RING, 0:n], raw[:, s % RAW, u % 2, 0:n],
                    w_hi[:, u % RING, 0:n]).then_inc(lo_ready, 1)

            def slot(u, off=0):
                if u + RING - 1 < 2 * SLABS:
                    split_lo(u + RING - 1, off)

            def unit_done(u, off=0):
                dve.wait_ge(unit_used, u + 1 + off)

            def begin_norm(name):
                if NORM[name] > 0:
                    dve.wait_ge(ss_ready, NORM[name])
                dve.memset(acc[:, :], 0.0).then_inc(acc_clear, 1)
                dve.wait_ge(acc_clear, NORM[name] + 1)

            def add(n, c, off=0):
                dve.wait_ge(sq_ready, c + 1 + off)
                if c > 0:
                    dve.wait_ge(acc_done, c + off)
                dve.tensor_tensor(acc[:, 0:n], acc[:, 0:n], sq[:, c % 2, 0:n], ALU.add).then_inc(acc_done, 1)

            def scale_lo(dst, src, g, hi, c, off=0):
                dve.wait_ge(xh_ready, c + 1 + off)
                dve.scalar_tensor_tensor(dst, src, g, hi.bitcast(F32), ALU.mult, ALU.subtract)\
                   .then_inc(xg_ready, 1)

            def make_rstd(name, dst, n):
                dve.wait_ge(root_ready, NORM[name] + 1)
                dve.reciprocal(dst[:, 0:n], root[:, 0:n]).then_inc(rstd_ready, 1)
                dve.wait_ge(rstd_ready, NORM[name] + 1)

            def row_maxima(a):
                buf, *parts = score_parts(a)
                i = 2 * (a % 2)
                dve.wait_ge(scores_ready, a + 1)
                if kind(a).startswith("mem"):
                    link(dve.tensor_reduce(row_max[:, i:i + 2], score_bank(a)[:, :].rearrange("p (t n) -> p t n", t=2),
                                           AX.X, ALU.max))
                else:
                    if a >= 2:
                        dve.wait_ge(pt_ready, a - 1)
                    mask = K_MASK1 if kind(a) == "forget" else K_MASK2
                    for t, (c, n) in enumerate(parts):
                        ins = dve.tensor_tensor_reduce(
                            out=buf[:, c:c + n], in0=score_bank(a)[:, c:c + n], in1=const[:, mask + c:mask + c + n],
                            scale=1.0, scalar=-3e38, op0=ALU.add, op1=ALU.max,
                            accum_out=row_max[:, i + t:i + t + 1])
                        if t == 1:
                            link(ins)
                dve.tensor_scalar(neg_max[:, i:i + 2], row_max[:, i:i + 2], -SCALE[kind(a)], None, ALU.mult)\
                   .then_inc(rowmax_ready, 1)

            def normalise(a):
                buf, *parts = score_parts(a)
                i = 2 * (a % 2)
                dve.wait_ge(exp_ready, 2 * a + 2)
                link(dve.reciprocal(row_inv[:, i:i + 2], row_sum[:, i:i + 2]))
                for t, (c, n) in enumerate(parts):
                    dve.tensor_scalar(buf[:, c:c + n], buf[:, c:c + n], row_inv[:, i + t:i + t + 1], None, ALU.mult)\
                       .then_inc(probs_ready, 1)

            def take_output(dst, a):
                dve.wait_ge(heads_done, a + 1)
                dve.tensor_copy(dst, side[2][:, 256:512]).then_inc(o_copied, 1)

            dve.memset(eps_c, EPS).then_inc(consts_set, 1)
            dve.memset(one_c, 1.0).then_inc(consts_set, 1)

            begin_norm("in1")
            dve.wait_ge(par_in, 16)
            for k in range(KC):
                dve.wait_ge(x0_in[k // (KC // 2)], 16)
                scale_lo(xg_lo[:, k, :], x0[:, k, :], gain("in1", k), xg_hi[:, k, :], k)
                add(TOK, k)
                if k == 0:
                    dve.wait_ge(small_hi, 1)
                    low(wf_lo[:, :], wf[:, :], wf_hi[:, :]).then_inc(small_lo, 1)
            for u in range(2):
                split_lo(u)
            make_rstd("in1", rstd, TOK)
            t0 = FIRST_TILE["in1"]
            dve.wait_ge(extra_done, 1)
            dve.tensor_tensor(lf[:, :], main[0][0:8, 0:TOK], rstd[0:8, 0:TOK], ALU.mult).then_inc(evac, 1)
            dve.wait_ge(evac, 1)
            dve.tensor_scalar(lf[:, :], lf[:, :], par[0:8, C_BF:C_BF + 1], None, ALU.add).then_inc(f_ready, 1)

            split_lo(2)

            def taken(dst, t, scale, rows=P, c=0):
                n = 1
                for s in dst.shape[1:]:
                    n *= s
                return dve.tensor_tensor(dst, main[t % 4][0:rows, c:c + n], scale, ALU.mult)

            for u in range(40):
                a = u - 12
                if a == 0:
                    dve.wait_ge(mask_in, 16)
                if 0 <= a < MEM_A:
                    row_maxima(a)
                if 0 <= a - 1 < MEM_A:
                    normalise(a - 1)
                if 0 < a - 3 < MEM_A and (a - 3) % 2 == 1:
                    take_output(o1[:, (a - 3) // 2, :], a - 3)
                if u == 4:
                    dve.wait_ge(f_act, 1)
                    dve.wait_ge(f_ready, 1)
                    link(dve.scalar_tensor_tensor(lf[:, :], lf[:, :], 0.0, lf2[:, :], ALU.min, ALU.subtract))
                    dve.wait_ge(const_in, 16)
                    link(dve.tensor_tensor_scan(c8[:, 0:P], ones[0:8, :], lf[:, 0:P], 0.0, ALU.mult, ALU.add))
                    link(dve.tensor_tensor_scan(c8[:, P:2 * P], ones[0:8, :], lf[:, P:2 * P], c8[:, P - 1:P],
                                                ALU.mult, ALU.add))
                    link(dve.tensor_tensor_scan(c8[:, 2 * P:TOK], ones[0:8, 0:TOK - 2 * P], lf[:, 2 * P:TOK],
                                                c8[:, 2 * P - 1:2 * P], ALU.mult, ALU.add))
                    dve.tensor_scalar(c8[:, :], c8[:, :], -float(HD1) ** 0.5, None, ALU.mult).then_inc(c_ready, 1)
                if u == 6:
                    dve.wait_ge(col_ready, 1)
                    dve.tensor_copy(rc1[0:META, 0:1], side[0][0:META, 0:1])
                    dve.tensor_copy(rc1[:, 1:3], side[0][:, 1:3]).then_inc(col_copied, 1)
                if u == 11:
                    unit_done(u)
                    dve.wait_ge(col_copied, 1)
                    for j in range(3):
                        n = META if j == 0 else P
                        dve.tensor_scalar(v1[0:n, j, :], main[(t0 + 8 + j) % 4][0:n, :], rc1[0:n, j:j + 1], None,
                                          ALU.mult).then_inc(evac, 1)
                if not 8 <= u < 12:
                    t = t0 + (u if u < 8 else u - 1)
                    unit_done(u)
                    late = rstd[:, META:TOK]
                    dst, scale = (
                        (q1[:, u % 4, :], late) if u < 4 else (k1[:, u % 4, :], rstd[:, 0:TOK]) if u < 8 else
                        (z_attn[:, u % 4, :], late) if u < 16 else (u1[:, u % 4, :], rstd[:, 0:TOK]) if u < 20 else
                        (z_pool[:, u % 4, :], late) if u < 24 else (gates[:, u % 8, (u - 24) // 8, :], late))
                    taken(dst, t, scale).then_inc(evac, 1)
                slot(u)
                if u == 23:
                    dve.wait_ge(pool_hi_ready, 1)
                    low(pool_lo[:, :, :], pooled[:, :, :], pool_hi[:, :, :]).then_inc(pool_split, 1)
                if u == 26:
                    dve.wait_ge(act_z, 1)
                    dve.wait_ge(o_copied, 4)
                    dve.tensor_tensor(y1[:, :, :], o1[:, :, :], z_attn[:, :, :], ALU.mult).then_inc(y_done, 1)
                if u == 28:
                    dve.wait_ge(y_hi_ready, 1)
                    low(y_lo[:, 4:8, :], y1[:, :, :], y_hi[:, 4:8, :]).then_inc(y_split, 1)
                if 29 <= u < 37:
                    if u == 29:
                        begin_norm("mem")
                    add(SEQ, SQ0["mem"] + u - 29)

            t0 = FIRST_TILE["pool"]
            dve.wait_ge(act_z, 2)
            for j in range(2):
                unit_done(first_unit("w_pool") + j)
                for g in (2 * j, 2 * j + 1):
                    dve.scalar_tensor_tensor(y1[:, g, :], main[(t0 + g) % 4][:, 0:SEQ], par[:, C_POOL + g:C_POOL + g + 1],
                                             z_pool[:, g, :], ALU.mult, ALU.mult).then_inc(evac, 1)
            dve.wait_ge(y_hi_ready, 2)
            low(y_lo[:, 0:4, :], y1[:, :, :], y_hi[:, 0:4, :]).then_inc(y_split, 1)
            for j in range(2):
                slot(first_unit("w_pool") + j)
            t0 = FIRST_TILE["up"]
            dve.wait_ge(act_z, 4)
            for m in range(KC):
                unit_done(first_unit("w_up") + m)
                dve.tensor_tensor(gated[:, m % 2, :], main[(t0 + m) % 4][:, :],
                                  gates[:, m, :, :].rearrange("p a n -> p (a n)"), ALU.mult).then_inc(evac, 1)
                if m >= 2:
                    dve.wait_ge(merged_hi, m - 1)
                dve.wait_ge(evac, t0 + m + 1)
                dve.tensor_tensor(merged[:, m % 2, :], gated[:, m % 2, 0:SEQ], gated[:, m % 2, SEQ:2 * SEQ],
                                  ALU.add).then_inc(sum_done, 1)
                if m < KC - 1:
                    slot(first_unit("w_up") + m)
                dve.wait_ge(merged_hi, m + 1)
                low(xg_lo[:, m, 0:SEQ], merged[:, m % 2, :], xg_hi[:, m, 0:SEQ]).then_inc(merged_split, 1)
            slot(first_unit("w_up") + KC - 1)
            make_rstd("mem", rstd_mem, SEQ)
            t0 = FIRST_TILE["out1"]
            begin_norm("end1")
            dve.wait_ge(x_in, 16)
            for m in range(KC):
                scale_lo(mem_lo[:, m, :], mem_x[:, m, :], gain("mem", m), mem_hi[:, m, :], XG0["mem"] + m)
                unit_done(first_unit("w_out1") + m)
                dve.tensor_tensor(x[:, m, :], main[(t0 + m) % 4][:, 0:SEQ], x[:, m, :], ALU.add).then_inc(evac, 1)
                if m < KC - 1:
                    slot(first_unit("w_out1") + m)
                add(SEQ, SQ0["end1"] + m)
            slot(first_unit("w_out1") + KC - 1)

            dve.wait_ge(col_ready, 2)
            dve.tensor_copy(rcm, side[0][:, 4:6]).then_inc(col_copied, 1)
            dve.wait_ge(col_copied, 2)
            t0 = FIRST_TILE["memkv"]

            def split_x(j):
                dve.wait_ge(x_new, j + 1)
                scale_lo(xg_lo[:, j, 0:SEQ], x[:, j, :], gain("ffn_a1", j), xg_hi[:, j, 0:SEQ], XG0["ffn_a1"] + j)
                add(SEQ, SQ0["ffn_a1"] + j)

            for j in range(KC):
                layer, part = j // 4, j % 4
                if j == 0:
                    make_rstd("end1", rstd, SEQ)
                    begin_norm("ffn_a1")
                for k in chunks_of(j):
                    dve.scalar_tensor_tensor(x[:, k, :], x[:, k, :], gain("end1", k), rstd[:, 0:SEQ],
                                             ALU.mult, ALU.mult).then_inc(x_new, 1)
                if part < 2:
                    unit_done(first_unit("w_memkv") + j)
                    taken(mem_k[:, layer, part, :], t0 + j, rstd_mem[:, :]).then_inc(evac, 1)
                elif part == 3:
                    unit_done(first_unit("w_memkv") + j)
                    for i in range(2):
                        dve.tensor_scalar(mem_v[:, layer, i, :], main[(t0 + j - 1 + i) % 4][:, 0:SEQ],
                                          rcm[:, i:i + 1], None, ALU.mult).then_inc(evac, 1)
                slot(first_unit("w_memkv") + j)
                for k in chunks_of(j):
                    split_x(k)

            def residual(m, t, name, alpha, i, per, between=None):
                row = m if isinstance(i, int) else i * per + m
                off = 0 if isinstance(i, int) else i * per
                xm = x[:, row, :]
                dve.scalar_tensor_tensor(xm, main[(t + m) % 4][:, 0:SEQ], alpha, xm, ALU.mult, ALU.add).then_inc(evac, 1)
                if between:
                    between()
                if name != "end2":
                    dve.wait_ge(evac, t + m + 1 + off)
                    scale_lo(xg_lo[:, row, 0:SEQ], xm, gain(name, row), xg_hi[:, row, 0:SEQ],
                             XG0[name] + m, off)
                add(SEQ, SQ0[name] + m, off)

            def ffn(which):
                f, u0, t0 = FFNS.index(which), first_unit("w_gu_" + which), FIRST_TILE["gu_" + which]
                then = FFN_THEN[which]
                if which != "b1":
                    make_rstd(FFN_NORM[which], rstd, SEQ)

                def hidden(t, i=0):
                    tt = t if isinstance(i, int) else i * 4 + t
                    n, b = f * FT + t, 0 if isinstance(i, int) else i * 4
                    unit_done(u0 + 2 * t, i * 8)
                    taken(gate_n[:, t % 2, :], t0 + 2 * t, rstd[:, 0:SEQ]).then_inc(evac, 1)
                    slot(u0 + 2 * t, i * 8)
                    unit_done(u0 + 2 * t + 1, i * 8)
                    taken(hid[:, t % 2, :], t0 + 2 * t + 1, rstd[:, 0:SEQ]).then_inc(evac, 1)
                    dve.wait_ge(silu_ready, n + 1 + b)
                    dve.wait_ge(evac, t0 + 2 * t + 2 + i * 8)
                    dve.tensor_tensor(hid[:, t % 2, :], hid[:, t % 2, :], gate_s[:, t % 2, :], ALU.mult)\
                       .then_inc(hid_ready, 1)
                    slot(u0 + 2 * t + 1, i * 8)
                    dve.wait_ge(hid_ready, n + 1 + b)
                    dve.wait_ge(h_hi_ready, n + 1 + b)
                    low(h_lo[:, tt, :], hid[:, t % 2, :], h_hi[:, tt, :]).then_inc(h_ready, 1)

                with dve.Fori(0, FT // 4) as i:
                    for t in range(4):
                        hidden(t, i)
                for t in range(FT // 4 * 4, FT):
                    hidden(t)
                begin_norm(then)
                u0, t0 = first_unit("w_down_" + which), FIRST_TILE["down_" + which]

                def down(m, i=0):
                    slot(u0 + 2 * m, i * 8)
                    unit_done(u0 + 2 * m + 1, i * 8)
                    residual(m, t0, then, 0.5, i, 4)
                    slot(u0 + 2 * m + 1, i * 8)

                if which == "b2":
                    for m in range(KC):
                        down(m)
                else:
                    with dve.Fori(0, 2) as i:
                        for m in range(4):
                            down(m, i)

            def mix_out(name, then):
                u0 = first_unit("w_" + name)
                begin_norm(then)
                for m in range(KC):
                    unit_done(u0 + m)
                    split = lambda: slot(u0 + m)
                    residual(m, FIRST_TILE[name], then, 1.0, 0, 0, split if m < KC - 1 else None)
                slot(u0 + KC - 1)

            ffn("a1")

            u0, t0 = first_unit("w_in_a"), FIRST_TILE["in_a"]
            make_rstd("mix_a", rstd, SEQ)
            link(dve.memset(cx[:, :, 0:3], 0.0))

            def convolve(t, taps):
                for j in taps:
                    ins = dve.scalar_tensor_tensor(cy[:, t % 2, :], cx[:, t % 2, j:j + SEQ],
                                                   par[:, C_CONV + 4 * t + j:C_CONV + 4 * t + j + 1],
                                                   cy[:, t % 2, :], ALU.mult, ALU.add)
                    if j == 0:
                        ins.then_inc(conv_done, 1)
                    elif j == 1:
                        link(ins)
                    else:
                        ins.then_inc(tap_done, 1)

            for t in range(26):
                h = t - 21
                if 0 <= h < MEMH:
                    row_maxima(MEM_A + h)
                if 0 <= h - 1 < MEMH:
                    normalise(MEM_A + h - 1)
                if h == 4:
                    take_output(om_a[:, 0, :], MEM_A + 1)
                if t == 18:
                    dve.wait_ge(extra_done, 2)
                    bt = FIRST_TILE["ba"]
                    taken(ba[:, :], bt, rstd[0:38, 0:SEQ], 38).then_inc(evac, 1)
                    dve.wait_ge(evac, bt + 1)
                    dve.tensor_scalar(sp1[32:38, :], ba[32:38, :], par[32:38, C_DT:C_DT + 1], None, ALU.add)\
                       .then_inc(ba_dve, 1)
                unit_done(u0 + t)
                if t < 18:
                    if t >= 2:
                        dve.wait_ge(conv_done, t - 1)
                    taken(cx[:, t % 2, 3:3 + SEQ], t0 + t, rstd[:, 0:SEQ]).then_inc(evac, 1)
                else:
                    taken(qm_a[:, t - 18, :] if t < 20 else gate_a[:, t - 20, :], FIRST_TILE["in_a_tail"] + t - 18,
                          rstd[:, 0:SEQ]).then_inc(evac, 1)
                if 1 <= t <= 18:
                    dve.wait_ge(conv0, t)
                    convolve(t - 1, (2,))
                slot(u0 + t)
                if 1 <= t <= 18:
                    dve.wait_ge(tap_done, t)
                    convolve(t - 1, (1, 0))
                if t == 12:
                    dve.wait_ge(small_hi, 2)
                    low(wba_lo[:, :], wba[:, :], wba_hi[:, :]).then_inc(small_lo, 1)
                if t == 21:
                    dve.wait_ge(col_act, 1)
                    link(dve.reciprocal(cols[:, 80:104], cols[:, 184:208]))
                if t == 22:
                    dve.wait_ge(ba_act, 3)
                    soft = sp1[32:38, :]
                    link(dve.scalar_tensor_tensor(soft, soft, 0.0, sp2[32:38, :], ALU.max, ALU.add))
                    link(dve.tensor_scalar(soft, soft, small[32:38, 30:31], -1.0, ALU.mult, ALU.mult))
                    for c in (0, P):
                        ins = dve.tensor_tensor_scan(ba[32:38, c:c + P], ones[32:38, :], sp1[32:38, c:c + P], 0.0,
                                                     ALU.mult, ALU.add)
                    ins.then_inc(ba_dve, 1)
                if t == 24:
                    dve.wait_ge(ba_t, 1)
                    dve.tensor_copy(cols[:, 0:76], side[3][:, 128:204]).then_inc(col_copied, 1)
            take_output(om_a[:, 1, :], MEM_A + 3)

            dve.wait_ge(col_copied, 3)
            dve.wait_ge(col_act, 2)
            k_beta, q_scale = packed[:, :, 0:6], packed[:, :, 12:18]
            dve.tensor_tensor(k_beta, kq_inv[:, :, 0:6], b_col, ALU.mult)
            dve.tensor_copy(packed[:, :, 6:12], g_col)
            link(dve.tensor_scalar(q_scale, kq_inv[:, :, 6:12], DK ** -0.5, None, ALU.mult))
            dve.tensor_tensor(packed[:, :, 18:24], q_scale, e_g, ALU.mult)
            link(dve.tensor_tensor(k_neg, k_beta, e_g, ALU.mult))
            dve.tensor_scalar(k_neg, k_neg, -1.0, None, ALU.mult).then_inc(cpk_ready, 1)

            def split_rows(n):
                link(dve.tensor_copy(rows_hi[0:n, :], side[3][0:n, 256:512]))
                return low(rows_lo[0:n, :], side[3][0:n, 256:512], rows_hi[0:n, :])

            t0 = FIRST_TILE["vt"]
            for j in range(3):
                dve.wait_ge(turned_v, j + 1)
                for i in range(4):
                    h, c = 2 * j + i // 2, i % 2
                    ins = dve.tensor_scalar(kqv[:, 12 + h, c * P:(c + 1) * P], main[(t0 + j) % 4][:, i * P:(i + 1) * P],
                                            b_col[:, c, h:h + 1], None, ALU.mult)
                ins.then_inc(evac, 1)
                if j == 0:
                    dve.wait_ge(rows_t, 1)
                    split_rows(24).then_inc(rows_ready, 1)

            t0 = FIRST_TILE["delta"]
            for h in range(DH):
                b01, b23, ga = (main[(t0 + 3 * h + i) % 4] for i in range(3))
                d = h % 2
                dve.wait_ge(spread, 2 * h + 1)
                for c in range(2):
                    dve.scalar_tensor_tensor(dec[:, d, 0, c * P:(c + 1) * P], b01[:, SEQ + c * P:SEQ + (c + 1) * P],
                                             g_col[:, c, h:h + 1], const[:, K_CAUS:K_CAUS + P],
                                             ALU.subtract, ALU.add).then_inc(diff_ready, 1)
                dve.tensor_tensor(g_last[:, h:h + 1], b01[:, SEQ + P - 1:SEQ + P], g_col[:, 0, h:h + 1],
                                  ALU.subtract).then_inc(diff_ready, 1)
                dve.wait_ge(decay_ready, h + 1)
                dve.tensor_tensor(dec[:, d, 2, :], dec[:, d, 1, :], b01[:, 0:SEQ], ALU.mult).then_inc(evac, 1)
                dve.wait_ge(spread, 2 * h + 2)
                dve.tensor_tensor(dec[:, d, 3, :], dec[:, d, 1, :], b23[:, 0:SEQ], ALU.mult)
                dve.wait_ge(gram, h + 1)
                q_late = kqv[:, 6 + h, P:SEQ]
                dve.tensor_tensor(q_late, q_late, b23[:, SEQ + P:2 * SEQ], ALU.mult).then_inc(evac, 1)
                dve.wait_ge(evac, t0 + 3 * h + 2)
                for c in range(2):
                    for i, dst in enumerate((n_t, a_t)):
                        ins = dve.scalar_tensor_tensor(
                            dst[:, c * DH + h, :], ga[:, i * SEQ + c * P:i * SEQ + (c + 1) * P], kq_inv[:, c, h:h + 1],
                            dec[:, d, 2 + i, c * P:(c + 1) * P], ALU.mult, ALU.mult)
                ins.then_inc(evac, 1)
            dve.wait_ge(col_act, 3)
            link(dve.tensor_tensor(k_scale, g_last, kq_inv[:, 0, 0:6], ALU.mult))
            t0 = FIRST_TILE["kt"]
            for j, heads in enumerate(((0, 4), (4, 6))):
                dve.wait_ge(turned_k, j + 1)
                for h in range(*heads):
                    ins = dve.tensor_scalar(k_dec[:, h, :], main[(t0 + j) % 4][:, (h % 4) * P:(h % 4 + 1) * P],
                                            k_scale[:, h:h + 1], None, ALU.mult)
                ins.then_inc(evac, 1)

            for s in range(21):
                g = s % 3
                group = slice(4 * g, 4 * g + 4)
                if s < 3:
                    dve.wait_ge(c_masked, s + 1)
                    dve.tensor_tensor(d_t[:, group, :], ident.unsqueeze(1).to_broadcast([P, 4, P]),
                                      inv_c[:, s % 2, :].rearrange("p (n i) -> p n i", n=4), ALU.subtract)\
                       .then_inc(d_dve, 1)
                else:
                    n = s - 3
                    dve.wait_ge(dx_ready, n + 1)
                    d = d_lo if s < 18 else d_t
                    dve.tensor_tensor(d[:, group, :], d[:, group, :],
                                      main[2 + n % 2][:, :].rearrange("p (n i) -> p n i", n=4), ALU.subtract)\
                       .then_inc(d_dve, 1)

            def by_heads(dst, bank, heads, seen):
                a, b = heads
                dve.wait_ge(rec_pe, seen)
                dve.tensor_copy(dst, bank[:, 0:(b - a) * P].rearrange("p (h n) -> p h n", h=b - a))\
                   .then_inc(rec_dve, 1)

            halves = ((0, 4), (4, 6))
            for j, (a, b) in enumerate(halves):
                by_heads(state[:, a:b, :], main[2 + j], (a, b), 3 + j)
            for j, (a, b) in enumerate(halves):
                by_heads(o_a[:, a:b, 0:P], side[j], (a, b), 5 + j)
            for j, (a, b) in enumerate(halves):
                dve.wait_ge(rec_pe, 7 + j)
                for h in range(a, b):
                    dve.scalar_tensor_tensor(rhs1[:, h, :], main[j][:, (h - a) * P:(h - a + 1) * P],
                                             k_neg[:, 1, h:h + 1], kqv[:, 12 + h, P:SEQ], ALU.mult, ALU.add)\
                       .then_inc(rec_dve, 1)
            for j, (a, b) in enumerate(halves):
                by_heads(o_a[:, a:b, P:SEQ], side[j], (a, b), 11 + j)

            dve.wait_ge(og_act, 3)
            dve.reciprocal(o_inv, o_root).then_inc(og_dve, 1)
            dve.wait_ge(og_pe, 2)
            split_rows(6).then_inc(og_dve, 1)
            dve.wait_ge(cat_hi_ready, 1)
            low(cat_lo_a[:, 6:8, :], om_a[:, :, :], cat_hi_a[:, 6:8, :]).then_inc(cat_ready, 1)
            dve.wait_ge(gate_silu, 3)

            def output_lo(j):
                dve.wait_ge(cat_hi_ready, 2 + j)
                low(cat_lo_a[:, 2 * j:2 * j + 2, :], o_a[:, 2 * j:2 * j + 2, :], cat_hi_a[:, 2 * j:2 * j + 2, :])\
                    .then_inc(cat_ready, 1)

            for j in range(3):
                pair = o_a[:, 2 * j:2 * j + 2, :]
                dve.wait_ge(og_pe, 3 + j)
                dve.scalar_tensor_tensor(pair, pair, par[:, C_OUTG:C_OUTG + 1],
                                         scale_bank(j)[:, :].rearrange("p (h n) -> p h n", h=2), ALU.mult, ALU.mult)\
                   .then_inc(og_dve, 1)
                dve.wait_ge(og_dve, 3 + 2 * j)
                dve.tensor_tensor(pair, pair, gate_a[:, 2 * j:2 * j + 2, :], ALU.mult).then_inc(og_dve, 1)
                if j > 0:
                    output_lo(j - 1)
            output_lo(2)
            mix_out("out_a", "ffn_a2")
            ffn("a2")

            def latent(name, column):
                make_rstd(name, rstd_mem, SEQ)
                for j in range(2):
                    dve.scalar_tensor_tensor(lat[:, j, :], lat[:, j, :], par[:, column + j:column + j + 1],
                                             rstd_mem[:, :], ALU.mult, ALU.mult).then_inc(lat_done, 1)

            def latent_lo(n):
                dve.wait_ge(lat_hi_ready, n)
                low(lat_lo[:, :, :], lat[:, :, :], lat_hi[:, :, :]).then_inc(lat_ready, 1)

            def rotated(dst, plain, t, n):
                dve.wait_ge(extra_done, 2 + n)
                link(dve.tensor_tensor(dst, plain, cos[:, :], ALU.mult))
                taken(rot_s[:, :], t, sin[:, :]).then_inc(evac, 1)
                dve.wait_ge(evac, t + 1)
                dve.tensor_tensor(dst, dst, rot_s[:, :], ALU.add).then_inc(rope_ready, 1)

            make_rstd("kv", rstd, SEQ)
            begin_norm("kvlat")
            t0, u0 = FIRST_TILE["lat"], first_unit("w_lat")
            for j in range(2):
                unit_done(u0 + j)
                taken(lat[:, j, :], t0 + j, rstd[:, 0:SEQ]).then_inc(evac, 1)
                slot(u0 + j)
                add(SEQ, SQ0["kvlat"] + j)
            t0, u0 = FIRST_TILE["krope"], first_unit("w_krope")
            for j in range(2):
                slot(u0 + j)
            unit_done(u0 + 1)
            taken(rot_s[:, :], t0, rstd[:, 0:SEQ]).then_inc(evac, 1)
            latent("kvlat", C_KVLAT)
            latent_lo(1)
            dve.wait_ge(trig, 2)
            rotated(k_rope[:, :], rot_s[:, :], FIRST_TILE["krot"], 1)
            def next_lo(*chunks):
                for k in chunks:
                    scale_lo(xg_lo[:, k, 0:SEQ], x[:, k, :], gain("ffn_b1", k), xg_hi[:, k, 0:SEQ], XG0["ffn_b1"] + k)

            t0, u0 = FIRST_TILE["knope"], first_unit("w_knope")
            for j in range(2):
                unit_done(u0 + j)
                for h in range(3 * j, 3 * j + 3):
                    dve.tensor_copy(k_nope[:, h, :], main[(t0 + h) % 4][:, 0:SEQ]).then_inc(evac, 1)
                slot(u0 + j)
                next_lo(2 * j, 2 * j + 1)
            t0, u0 = FIRST_TILE["vmla"], first_unit("w_vmla")
            slot(u0)
            next_lo(4)
            unit_done(u0 + 1)
            for i in range(4):
                c, n = (0, 512) if i % 2 == 0 else (512, 256)
                dve.tensor_copy(v_mla[:, i // 2, c:c + n], main[(t0 + i) % 4][:, 0:n]).then_inc(evac, 1)
            next_lo(5, 6)
            slot(u0 + 1)
            next_lo(7)
            ffn("b1")

            make_rstd("mix_b", rstd, SEQ)
            begin_norm("qlat")
            t0, u0 = FIRST_TILE["in_b"], first_unit("w_in_b")
            for j in range(4):
                unit_done(u0 + j)
                taken(lat[:, j, :] if j < 2 else qm_b[:, j - 2, :], t0 + j, rstd[:, 0:SEQ]).then_inc(evac, 1)
                slot(u0 + j)
                if j < 2:
                    add(SEQ, SQ0["qlat"] + j)
            row_maxima(MEM_B)
            latent("qlat", C_QLAT)

            def query_unit(j):
                u = first_unit("w_qnope") + j
                if j < 4:
                    unit_done(u)
                if j < 2:
                    for h in range(3 * j, 3 * j + 3):
                        dve.tensor_copy(q_nope[:, h, :], main[(FIRST_TILE["qnope"] + h) % 4][:, 0:SEQ])\
                           .then_inc(evac, 1)
                elif j < 4:
                    for i in ((0,), (1, 2))[j - 2]:
                        dve.tensor_copy(q_rope[:, i, :], main[(FIRST_TILE["qrope"] + i) % 4][:, 0:SEQ])\
                           .then_inc(evac, 1)
                else:
                    for i in range(3):
                        rotated(q_rope[:, i, :], q_rope[:, i, :], FIRST_TILE["qrot"] + i, 2 + i)
                if j < 4:
                    slot(u)

            for i in range(MEMH + 3):
                if 1 <= i < MEMH:
                    row_maxima(MEM_B + i)
                if 0 <= i - 1 < MEMH:
                    normalise(MEM_B + i - 1)
                if i == 0:
                    latent_lo(2)
                if 1 <= i <= 5:
                    query_unit(i - 1)
                if i in (4, 6):
                    take_output(o_b[:, 6 + (i - 4) // 2, :], MEM_B + i - 3)
            for i in range(DH + 4):
                if i < DH:
                    row_maxima(MLA + i)
                if 0 <= i - 1 < DH:
                    normalise(MLA + i - 1)
                if 0 <= i - 3 < DH:
                    take_output(o_b[:, i - 3, :], MLA + i - 3)
                if i == 1:
                    dve.wait_ge(cat_hi_ready, 5)
                    low(cat_lo_b[:, 6:8, :], o_b[:, 6:8, :], cat_hi_b[:, 6:8, :]).then_inc(cat_ready, 1)
                if i >= 4:
                    dve.wait_ge(cat_hi_ready, 6 + i - 4)
                    low(cat_lo_b[:, i - 4, :], o_b[:, i - 4, :], cat_hi_b[:, i - 4, :]).then_inc(cat_ready, 1)
            mix_out("out_b", "ffn_b2")
            ffn("b2")
            make_rstd("end2", rstd, SEQ)
            for m in range(KC):
                dve.scalar_tensor_tensor(x[:, m, :], x[:, m, :], gain("end2", m), rstd[:, 0:SEQ], ALU.mult, ALU.mult)\
                   .then_inc(out_ready, 1)

        @block.gpsimd
        def _(gp):
            done = 0

            def link(ins):
                nonlocal done
                done += 1
                ins.then_inc(pool_chain, 1)
                gp.wait_ge(pool_chain, done)

            gp.wait_ge(par_in, 16)
            gp.wait_ge(pos_in, 16)
            angle, turns, part_of = y1[:, 1, :], y1[:, 2, :], y1[:, 3, :]
            link(gp.tensor_copy(y1[:, 0, :], pos[:, :]))
            link(gp.tensor_scalar(angle, y1[:, 0, :], par[:, C_INV:C_INV + 1], None, ALU.mult))
            for dst, quarter in ((ang, 0.25), (turn, 0.0)):
                link(gp.tensor_scalar(turns, angle, 1.0 / TWO_PI, quarter, ALU.mult, ALU.add))
                link(gp.tensor_scalar(turns, turns, ROUNDER, None, ALU.add))
                link(gp.tensor_scalar(turns, turns, -ROUNDER, None, ALU.add))
                src = angle
                for part in TWO_PI_PARTS:
                    link(gp.tensor_scalar(part_of, turns, part, None, ALU.mult))
                    link(gp.tensor_tensor(dst[:, :], src, part_of, ALU.subtract))
                    src = dst[:, :]
                link(gp.tensor_scalar(dst[:, :], dst[:, :], quarter * TWO_PI, PI_DOWN, ALU.add, ALU.min))
                gp.tensor_scalar(dst[:, :], dst[:, :], -PI_DOWN, None, ALU.max).then_inc(ang_ready, 1)

            for g in range(4):
                gp.wait_ge(evac, FIRST_TILE["in1"] + 15 + g + 1)
                src = u1[:, g, :]
                for level in range(g + 1):
                    back = 2 ** level
                    first = 2 * back - 1
                    dst = pool_tmp[:, level % 2, :]
                    link(gp.tensor_tensor(dst[:, first:TOK], src[:, first:TOK], src[:, first - back:TOK - back],
                                          ALU.add))
                    src = dst
                link(gp.tensor_scalar(pooled[:, g, :], src[:, META:TOK], 0.5 ** (g + 1), None, ALU.mult))
                gp.tensor_tensor(pooled[:, g, :], pooled[:, g, :], u1[:, g, META:TOK], ALU.subtract)\
                  .then_inc(pooled_ready, 1)
            gp.wait_ge(mask_in, 16)
            gp.wait_ge(evac, FIRST_TILE["kt"])
            for s in range(21):
                level, g = s // 3, s % 3
                if 2 <= s < 5:
                    gp.wait_ge(d_dve, s - 1)
                elif s >= 5:
                    gp.wait_ge(x_ready, s - 4)
                mask = const[:, K_LEV + level * P:K_LEV + (level + 1) * P]
                gp.tensor_tensor(inv_c[:, s % 2, :].rearrange("p (n i) -> p n i", n=4), n_t[:, 4 * g:4 * g + 4, :],
                                 mask.unsqueeze(1).to_broadcast([P, 4, P]), ALU.mult).then_inc(c_masked, 1)

        @block.tensor
        def _(pe):
            def bank_of(t, off=0):
                if t >= 4:
                    pe.wait_ge(evac, t - 3 + off)
                return main[t % 4]

            def triple(dst, a_hi, a_lo, b_hi, b_lo, first, last):
                pe.matmul(dst, a_hi, b_hi, start=first, stop=False)
                pe.matmul(dst, a_lo, b_hi, start=False, stop=False)
                return pe.matmul(dst, a_hi, b_lo, start=False, stop=last)

            def unit_begin(u, off=0):
                pe.wait_ge(lo_ready, u + 1 + off)

            def unit_end(ins):
                ins.then_inc(unit_used, 1)

            def project(u, dst, hi, lo, off=0, first=None):
                unit_begin(u, off)
                for k in range(KC):
                    if first is not None:
                        pe.wait_ge(xg_ready, first + k + 1)
                    ins = triple(dst, piece(w_hi, u, k), piece(w_lo, u, k), hi[:, k], lo[:, k], k == 0, k == KC - 1)
                unit_end(ins)

            xs_hi, xs_lo = xg_hi[:, :, 0:SEQ], xg_lo[:, :, 0:SEQ]

            def norm_sum(name, n=SEQ):
                pe.wait_ge(acc_done, SQ0[name] + dict(NORMS)[name])
                if NORM[name] > 0:
                    pe.wait_ge(root_ready, NORM[name])
                pe.matmul(side[3][:, 0:n], ones, acc[:, 0:n], start=True, stop=True).then_inc(ss_ready, 1)

            def scores(a):
                last = a - 2 if a >= MEM_B + 2 else a - 1
                if a == MEM_B + 1:
                    pe.wait_ge(root_ready, NORM["qlat"] + 1)
                if last >= 0 and kind(last).startswith("mem"):
                    pe.wait_ge(exp_ready, 2 * last + 2)
                elif last >= 0:
                    pe.wait_ge(rowmax_ready, last + 1)
                which, (_, *parts) = kind(a), score_parts(a)
                for t, (c, n) in enumerate(parts):
                    dst, q = score_bank(a)[:, c:c + n], slice(t * P, (t + 1) * P)
                    if which == "mla":
                        h = a - MLA
                        pe.matmul(dst, q_nope[:, h, q], k_nope[:, h, 0:n], start=True, stop=False)
                        r = slice(64 * (h % 2), 64 * (h % 2) + 64)
                        ins = pe.matmul(dst, q_rope[r, h // 2, q], k_rope[r, 0:n], start=False, stop=True)
                    elif which == "forget":
                        r, h = slice(64 * (a % 2), 64 * (a % 2) + 64), a
                        pe.matmul(dst, q1[r, h // 2, q], k1[r, h // 2, 0:n], start=True, stop=False)
                        ins = pe.matmul(dst, ident[0:8, h:h + 1].to_broadcast([8, P]), c8[:, 0:n],
                                        start=False, stop=True)
                    else:
                        h, layer, qm = (a - MEM_A, 0, qm_a) if which == "mem_a" else (a - MEM_B, 1, qm_b)
                        r = slice(64 * (h % 2), 64 * (h % 2) + 64)
                        ins = pe.matmul(dst, qm[r, h // 2, q], mem_k[r, layer, h // 2, :], start=True, stop=True)
                ins.then_inc(scores_ready, 1)

            def turn_probs(a):
                pe.wait_ge(probs_ready, 2 * a + 2)
                if a > 0:
                    pe.wait_ge(pt_copied, copies_before(a))
                buf, *parts = score_parts(a)
                for key, keys, first, bank, col, _ in key_blocks(a):
                    for t in range(first, 2):
                        c = parts[t][0] + key
                        ins = pe.transpose(bank[0:keys, col + (t - first) * P:col + (t - first + 1) * P],
                                           buf[:, c:c + keys], ident)
                ins.then_inc(pt_ready, 1)

            def outputs(a):
                pe.wait_ge(pt_copied, copies_before(a + 1))
                which = kind(a)
                if a > 0 and outputs_before(a) > 0 and (which == "mla" or a % 2 == 0):
                    pe.wait_ge(o_copied, outputs_before(a))
                blocks = key_blocks(a)
                if which == "forget":
                    blocks = [blocks[0], blocks[2], blocks[1]]
                width = P if which == "mla" else 64
                r = 0 if which == "mla" else 64 * (a % 2)
                for n, (key, keys, first, _, _, col) in enumerate(blocks):
                    if which == "forget":
                        v = v1[0:keys, (key + P - META) // P if key else 0, a * 64:a * 64 + 64]
                    elif which == "mla":
                        v = v_mla[:, key // P, (a - MLA) * P:(a - MLA + 1) * P]
                    else:
                        h, layer = (a - MEM_A, 0) if which == "mem_a" else (a - MEM_B, 1)
                        v = mem_v[:, layer, key // P, h * 64:h * 64 + 64]
                    q = (2 - first) * P
                    ins = pe.matmul(side[2][r:r + width, SEQ + first * P:2 * SEQ], v, probs_t(a)[0:keys, col:col + q],
                                    start=n == 0, stop=n == len(blocks) - 1)
                ins.then_inc(heads_done, 1)

            pe.wait_ge(const_in, 16)
            bank = bank_of(0)
            pe.wait_ge(small_lo, 1)
            for k in range(KC):
                pe.wait_ge(xg_ready, k + 1)
                w = slice(k * 8, k * 8 + P)
                ins = triple(bank[:, 0:TOK], wf_hi[:, w], wf_lo[:, w], xg_hi[:, k, :], xg_lo[:, k, :],
                             k == 0, k == KC - 1)
            ins.then_inc(extra_done, 1)
            norm_sum("in1", TOK)

            t0 = FIRST_TILE["in1"]
            for u in range(40):
                a = u - 12
                if a == 0:
                    pe.wait_ge(evac, t0 + 8)
                    pe.wait_ge(c_ready, 1)
                if 0 <= a < MEM_A:
                    scores(a)
                if 8 <= u < 12:
                    j = u - 8
                    if j == 0:
                        for i in range(3):
                            bank_of(t0 + 8 + i)
                    unit_begin(u)
                    for i, tok in enumerate((0, META, META + P)):
                        for kk in range(2):
                            k = 2 * j + kk
                            x_t = slice(tok, tok + P)
                            ins = triple(main[(t0 + 8 + i) % 4][:, :], xg_hi[:, k, x_t], xg_lo[:, k, x_t],
                                         piece(w_hi, u, 4 * kk, 4), piece(w_lo, u, 4 * kk, 4),
                                         k == 0, k == KC - 1)
                    unit_end(ins)
                else:
                    first = 0 if 4 <= u < 8 or 16 <= u < 20 else META
                    bank = bank_of(t0 + (u if u < 8 else u - 1))
                    project(u, bank[:, 0:TOK - first], xg_hi[:, :, first:TOK], xg_lo[:, :, first:TOK])
                if u == 4:
                    pe.wait_ge(rstd_ready, 1)
                    for j, (tok, n) in enumerate(((0, META), (META, P), (META + P, P))):
                        ins = pe.matmul(side[0][0:n, j:j + 1], rstd[:, tok:tok + n], ident[:, 0:1],
                                        start=True, stop=True)
                    ins.then_inc(col_ready, 1)
                if 0 <= a - 1 < MEM_A:
                    turn_probs(a - 1)
                if 0 <= a - 2 < MEM_A:
                    if a == 2:
                        pe.wait_ge(evac, t0 + 11)
                    outputs(a - 2)

            t0, u0 = FIRST_TILE["pool"], first_unit("w_pool")
            pe.wait_ge(pool_split, 1)
            for j in range(2):
                banks = [bank_of(t0 + g) for g in (2 * j, 2 * j + 1)]
                unit_begin(u0 + j)
                for i, bank in enumerate(banks):
                    g = 2 * j + i
                    ins = triple(bank[:, 0:SEQ], piece(w_hi, u0 + j, i), piece(w_lo, u0 + j, i),
                                 pool_hi[:, g, :], pool_lo[:, g, :], True, True)
                unit_end(ins)
                if j == 0:
                    norm_sum("mem")
            t0, u0 = FIRST_TILE["up"], first_unit("w_up")
            pe.wait_ge(y_split, 1)
            for m in range(KC):
                bank, u = bank_of(t0 + m), u0 + m
                unit_begin(u)
                for b in (4, 5, 6, 7, 0, 1, 2, 3):
                    if m == 0 and b == 0:
                        pe.wait_ge(y_split, 2)
                    ins = triple(bank[:, b // 4 * SEQ:(b // 4 + 1) * SEQ], piece(w_hi, u, b), piece(w_lo, u, b),
                                 y_hi[:, b, :], y_lo[:, b, :], b % 4 == 0, b % 4 == 3)
                unit_end(ins)
            t0, u0 = FIRST_TILE["out1"], first_unit("w_out1")
            for m in range(KC):
                bank = bank_of(t0 + m)
                unit_begin(u0 + m)
                for k in range(KC):
                    if m == 0:
                        pe.wait_ge(merged_split, k + 1)
                    ins = triple(bank[:, 0:SEQ], piece(w_hi, u0 + m, k), piece(w_lo, u0 + m, k),
                                 xs_hi[:, k], xs_lo[:, k], k == 0, k == KC - 1)
                unit_end(ins)
            pe.wait_ge(rstd_ready, NORM["mem"] + 1)
            for i in range(2):
                ins = pe.matmul(side[0][:, 4 + i:5 + i], rstd_mem[:, i * P:(i + 1) * P], ident[:, 0:1],
                                start=True, stop=True)
            ins.then_inc(col_ready, 1)

            t0, u0 = FIRST_TILE["memkv"], first_unit("w_memkv")
            for layer in range(2):
                for j in range(2):
                    t = t0 + 4 * layer + j
                    project(u0 + 4 * layer + j, bank_of(t)[:, 0:SEQ], mem_hi, mem_lo, 0,
                            XG0["mem"] if t == t0 else None)
                    if t == t0:
                        norm_sum("end1")
                t = t0 + 4 * layer + 2
                banks = [bank_of(t + i) for i in range(2)]
                for j in range(2):
                    u = u0 + 4 * layer + 2 + j
                    unit_begin(u)
                    for i, bank in enumerate(banks):
                        for kk in range(4):
                            k, tok = 4 * j + kk, slice(i * P, (i + 1) * P)
                            ins = triple(bank[:, 0:SEQ], mem_hi[:, k, tok], mem_lo[:, k, tok],
                                         piece(w_hi, u, 2 * kk, 2), piece(w_lo, u, 2 * kk, 2), k == 0, k == KC - 1)
                    unit_end(ins)

            def ffn(which):
                f, u0, t0 = FFNS.index(which), first_unit("w_gu_" + which), FIRST_TILE["gu_" + which]

                def turn(i, first=None):
                    for j in range(4):
                        project(u0 + j, bank_of(t0 + j, i * 4)[:, 0:SEQ], xs_hi, xs_lo, i * 4,
                                first if j == 0 else None)
                        if first is not None and j == 0 and which != "b1":
                            norm_sum(FFN_NORM[which])

                turn(0, XG0["ffn_" + which])
                with pe.Fori(1, 2 * FT // 4) as i:
                    turn(i)
                u0, t0 = first_unit("w_down_" + which), FIRST_TILE["down_" + which]
                with pe.Fori(0, 2) as i:
                    for m in range(4):
                        bank = bank_of(t0 + m, i * 4)
                        for j in range(2):
                            u = u0 + 2 * m + j
                            pe.wait_ge(h_ready, f * FT + FT // 2 * (j + 1))
                            unit_begin(u, i * 8)
                            for b in range(FT // 2):
                                k = j * (FT // 2) + b
                                ins = triple(bank[:, 0:SEQ], piece(w_hi, u, b), piece(w_lo, u, b),
                                             h_hi[:, k, :], h_lo[:, k, :], k == 0, k == FT - 1)
                            unit_end(ins)

            def mix_out(name, hi, lo, ready):
                order = sorted(range(KC), key=lambda k: ready[k])
                for m in range(KC):
                    u, bank = first_unit("w_" + name) + m, bank_of(FIRST_TILE[name] + m)
                    unit_begin(u)
                    for n, k in enumerate(order):
                        if m == 0:
                            pe.wait_ge(cat_ready, ready[k])
                        ins = triple(bank[:, 0:SEQ], piece(w_hi, u, k), piece(w_lo, u, k), hi[:, k], lo[:, k],
                                     n == 0, n == KC - 1)
                    unit_end(ins)

            ffn("a1")

            t0, u0 = FIRST_TILE["in_a"], first_unit("w_in_a")
            for t in range(26):
                h = t - 21
                if h == 0:
                    pe.wait_ge(evac, FIRST_TILE["in_a_tail"] + 2)
                if 0 <= h < MEMH:
                    scores(MEM_A + h)
                tile = t0 + t if t < 18 else FIRST_TILE["in_a_tail"] + t - 18
                project(u0 + t, bank_of(tile)[:, 0:SEQ], xs_hi, xs_lo, 0, XG0["mix_a"] if t == 0 else None)
                if t == 0:
                    norm_sum("mix_a")
                if 3 <= t < 15:
                    if t == 3:
                        pe.wait_ge(root_ready, NORM["mix_a"] + 1)
                    n = t - 3
                    pe.wait_ge(csq_ready, n + 1)
                    for c in range(2):
                        ins = pe.matmul(side[3][:, c * 12 + n:c * 12 + n + 1], csq[:, n % 2, c * P:(c + 1) * P],
                                        ones[:, 0:1], start=True, stop=True)
                    ins.then_inc(csum, 1)
                if t == 17:
                    bank = bank_of(FIRST_TILE["ba"])
                    pe.wait_ge(small_lo, 2)
                    for k in range(KC):
                        w = slice(k * 38, k * 38 + P)
                        ins = triple(bank[:, 0:SEQ], wba_hi[:, w], wba_lo[:, w], xs_hi[:, k], xs_lo[:, k],
                                     k == 0, k == KC - 1)
                    ins.then_inc(extra_done, 1)
                if t == 23:
                    pe.wait_ge(ba_dve, 2)
                    for c in range(2):
                        ins = pe.transpose(side[3][:, P + 38 * c:P + 38 * (c + 1)], ba[:, c * P:(c + 1) * P],
                                           ident[0:38, 0:38])
                    ins.then_inc(ba_t, 1)
                if 0 <= h - 1 < MEMH:
                    turn_probs(MEM_A + h - 1)
                if 0 <= h - 2 < MEMH:
                    outputs(MEM_A + h - 2)

            outputs(MEM_A + 3)

            t0 = FIRST_TILE["vt"]
            pe.wait_ge(csilu, 18)
            for j in range(3):
                bank = bank_of(t0 + j)
                for i in range(4):
                    ins = pe.transpose(bank[:, i * P:(i + 1) * P],
                                       kqv[:, 12 + 2 * j + i // 2, i % 2 * P:(i % 2 + 1) * P], ident)
                ins.then_inc(turned_v, 1)
                if j == 0:
                    pe.wait_ge(cpk_ready, 1)
                    for c in range(2):
                        ins = pe.transpose(side[3][0:24, 256 + c * P:256 + (c + 1) * P], cols[:, 104 + 24 * c:128 + 24 * c],
                                           ident)
                    ins.then_inc(rows_t, 1)

            def along_rows(dst, row, n=24):
                pick = ident_r[0:n, row:row + 1].to_broadcast([n, P])
                pe.matmul(dst, pick, rows_hi[0:n, :], start=True, stop=False)
                return pe.matmul(dst, pick, rows_lo[0:n, :], start=False, stop=True)

            t0 = FIRST_TILE["delta"]
            pe.wait_ge(ident_ready, 1)
            pe.wait_ge(rows_ready, 1)
            chunks = (slice(0, P), slice(P, SEQ))
            for h in range(DH):
                for i, (r0, r1) in enumerate(((h, 6 + h), (12 + h, 18 + h))):
                    bank = bank_of(t0 + 3 * h + i)
                    along_rows(bank[:, 0:SEQ], r0)
                    along_rows(bank[:, SEQ:2 * SEQ], r1).then_inc(spread, 1)
                bank = bank_of(t0 + 3 * h + 2)
                for i, other in enumerate((h, 6 + h)):
                    for c in range(2):
                        ins = pe.matmul(bank[:, (2 * i + c) * P:(2 * i + c + 1) * P], kqv[:, h, chunks[c]],
                                        kqv[:, other, chunks[c]], start=True, stop=True)
                ins.then_inc(gram, 1)
            t0 = FIRST_TILE["kt"]
            for j, (a, b) in enumerate(((0, 4), (4, 6))):
                bank = bank_of(t0 + j)
                for h in range(a, b):
                    ins = pe.transpose(bank[:, (h - a) * P:(h - a + 1) * P], kqv[:, h, 0:P], ident)
                ins.then_inc(turned_k, 1)


            def product(dst, lhs, rhs):
                for i in range(4):
                    c = slice(i * P, (i + 1) * P)
                    ins = pe.matmul(dst[:, c], lhs(i), rhs(i), start=True, stop=True)
                return ins

            for s in range(23):
                if 3 <= s < 21:
                    n, g = s - 3, s % 3
                    if n == 0:
                        pe.wait_ge(evac, t0 + 2)
                    pe.wait_ge(c_masked, s + 1)
                    if n < 3:
                        pe.wait_ge(turn_copied, n + 1)
                    else:
                        pe.wait_ge(d_dve, n + 1)
                    if n >= 2:
                        pe.wait_ge(x_copied, n - 1)
                    product(main[n % 2], lambda i: inv_c[:, s % 2, i * P:(i + 1) * P],
                            lambda i: d_lo[:, 4 * g + i, :]).then_inc(x_ready, 1)
                if 3 <= s - 1 < 21:
                    n, g = s - 4, (s - 1) % 3
                    pe.wait_ge(x_copied, n + 1)
                    if n < 3:
                        pe.wait_ge(d_dve, n + 1)
                    else:
                        pe.wait_ge(turn_copied, n + 1)
                    if n >= 2:
                        pe.wait_ge(d_dve, n + 2)
                    d = lambda i: d_t[:, 4 * g + i, :]
                    xx = lambda i: inv_x[:, n % 2, i * P:(i + 1) * P]
                    if s - 1 < 18:
                        product(main[2 + n % 2], d, xx).then_inc(dx_ready, 1)
                    else:
                        product(main[2 + n % 2], xx, d).then_inc(dx_ready, 1)
                for n in ([s] if s < 3 else []) + ([s - 2] if 3 <= s - 2 < 18 else []):
                    pe.wait_ge(d_dve, n + 1)
                    if n >= 2:
                        pe.wait_ge(turn_copied, n - 1)
                    g, src = n % 3, d_t if n < 3 else d_lo
                    for i in range(4):
                        ins = pe.transpose(side[n % 2][:, i * P:(i + 1) * P], src[:, 4 * g + i, :], ident)
                    ins.then_inc(turned, 1)

            halves = ((0, 4), (4, 6))

            def each(banks, parts, waits=((), ())):
                for j, (a, b) in enumerate(halves):
                    for sem_, value in waits[j]:
                        pe.wait_ge(sem_, value)
                    for h in range(a, b):
                        dst = banks[j][:, (h - a) * P:(h - a + 1) * P]
                        for n, (lhs, rhs) in enumerate(parts):
                            ins = pe.matmul(dst, lhs(h), rhs(h), start=n == 0, stop=n == len(parts) - 1)
                    ins.then_inc(rec_pe, 1)

            pe.wait_ge(d_dve, 21)
            each(main[0:2], [(lambda h: d_t[:, h, :], lambda h: kqv[:, 12 + h, 0:P])])
            each(main[2:4], [(lambda h: k_dec[:, h, :], lambda h: vn0[:, h, :])],
                 (((rec_act, 1),), ((rec_act, 2),)))
            each(side[0:2], [(lambda h: vn0[:, h, :], lambda h: a_t[:, h, :])], (((turn_copied, 18),), ()))
            each(main[0:2], [(lambda h: kqv[:, h, P:SEQ], lambda h: state[:, h, :])],
                 (((rec_dve, 1),), ((rec_dve, 2),)))
            each(main[2:4], [(lambda h: d_t[:, DH + h, :], lambda h: rhs1[:, h, :])],
                 (((rec_dve, 8),), ((rec_dve, 10),)))
            each(side[0:2], [(lambda h: vn1[:, h, :], lambda h: a_t[:, DH + h, :]),
                             (lambda h: state[:, h, :], lambda h: kqv[:, 6 + h, P:SEQ])],
                 (((rec_act, 3),), ((rec_act, 4),)))

            for c in range(2):
                pe.wait_ge(og_act, c + 1)
                for h in range(DH):
                    ins = pe.matmul(side[3][:, c * DH + h:c * DH + h + 1], osq[c][:, h, :], ones[:, 0:1],
                                    start=True, stop=True)
            ins.then_inc(og_pe, 1)
            pe.wait_ge(og_dve, 1)
            for c in range(2):
                ins = pe.transpose(side[3][0:6, 256 + c * P:256 + (c + 1) * P], cols[:, 220 + 6 * c:226 + 6 * c], ident)
            ins.then_inc(og_pe, 1)
            pe.wait_ge(og_dve, 2)
            for j in range(3):
                bank = scale_bank(j)
                along_rows(bank[:, 0:SEQ], 2 * j, 6)
                along_rows(bank[:, SEQ:2 * SEQ], 2 * j + 1, 6).then_inc(og_pe, 1)
            mix_out("out_a", cat_hi_a, cat_lo_a, [2, 2, 3, 3, 4, 4, 1, 1])
            ffn("a2")

            t0, u0 = FIRST_TILE["lat"], first_unit("w_lat")
            for j in range(2):
                project(u0 + j, bank_of(t0 + j)[:, 0:SEQ], xs_hi, xs_lo, 0, XG0["kv"] if j == 0 else None)
                if j == 0:
                    norm_sum("kv")
            u0, bank = first_unit("w_krope"), bank_of(FIRST_TILE["krope"])
            for j in range(2):
                unit_begin(u0 + j)
                for b in range(4):
                    k = 4 * j + b
                    ins = triple(bank[:, 0:SEQ], piece(w_hi, u0 + j, b), piece(w_lo, u0 + j, b),
                                 xs_hi[:, k], xs_lo[:, k], k == 0, k == KC - 1)
                unit_end(ins)
            norm_sum("kvlat")

            def rotate(t, src, ready):
                bank = bank_of(t)
                pe.wait_ge(evac, ready)
                pe.matmul(bank[:, 0:SEQ], rot, src, start=True, stop=True).then_inc(extra_done, 1)

            def three_tiles(u, t):
                banks = [bank_of(t + i) for i in range(3)]
                unit_begin(u)
                for i, bank in enumerate(banks):
                    for k in range(2):
                        ins = triple(bank[:, 0:SEQ], piece(w_hi, u, 2 * i + k), piece(w_lo, u, 2 * i + k),
                                     lat_hi[:, k, :], lat_lo[:, k, :], k == 0, k == 1)
                unit_end(ins)

            t = FIRST_TILE["krot"]
            rotate(t, rot_s[:, :], t)
            pe.wait_ge(lat_ready, 1)
            for j in range(2):
                three_tiles(first_unit("w_knope") + j, FIRST_TILE["knope"] + 3 * j)
            t0, u0 = FIRST_TILE["vmla"], first_unit("w_vmla")
            banks = [bank_of(t0 + i) for i in range(4)]
            for k in range(2):
                unit_begin(u0 + k)
                for i, bank in enumerate(banks):
                    b, n = (0, 4) if i % 2 == 0 else (4, 2)
                    tok = slice(i // 2 * P, (i // 2 + 1) * P)
                    ins = triple(bank[:, 0:n * P], lat_hi[:, k, tok], lat_lo[:, k, tok],
                                 piece(w_hi, u0 + k, b, n), piece(w_lo, u0 + k, b, n), k == 0, k == 1)
                unit_end(ins)
            ffn("b1")

            t0, u0 = FIRST_TILE["in_b"], first_unit("w_in_b")
            for j in range(4):
                project(u0 + j, bank_of(t0 + j)[:, 0:SEQ], xs_hi, xs_lo, 0, XG0["mix_b"] if j == 0 else None)
                if j == 0:
                    norm_sum("mix_b")
            norm_sum("qlat")
            pe.wait_ge(evac, t0 + 4)

            def query_unit(j):
                if j == 0:
                    pe.wait_ge(lat_ready, 2)
                if j < 2:
                    three_tiles(first_unit("w_qnope") + j, FIRST_TILE["qnope"] + 3 * j)
                elif j < 4:
                    u, t0 = first_unit("w_qrope") + j - 2, FIRST_TILE["qrope"]
                    banks = [bank_of(t0 + i) for i in range(3)]
                    unit_begin(u)
                    for b in range(3):
                        i, k = (3 * (j - 2) + b) // 2, (3 * (j - 2) + b) % 2
                        ins = triple(banks[i][:, 0:SEQ], piece(w_hi, u, b), piece(w_lo, u, b),
                                     lat_hi[:, k, :], lat_lo[:, k, :], k == 0, k == 1)
                    unit_end(ins)
                else:
                    for i in range(3):
                        rotate(FIRST_TILE["qrot"] + i, q_rope[:, i, :], FIRST_TILE["qrope"] + i + 1)

            for i in range(MEMH + 3):
                if i < MEMH:
                    scores(MEM_B + i)
                if 1 <= i <= 5:
                    query_unit(i - 1)
                if 0 <= i - 2 < MEMH:
                    turn_probs(MEM_B + i - 2)
                if 0 <= i - 3 < MEMH:
                    outputs(MEM_B + i - 3)
            pe.wait_ge(rope_ready, 4)
            for i in range(DH + 3):
                if i < DH:
                    scores(MLA + i)
                if 0 <= i - 2 < DH:
                    turn_probs(MLA + i - 2)
                if i >= 3:
                    outputs(MLA + i - 3)
            mix_out("out_b", cat_hi_b, cat_lo_b, [6, 7, 8, 9, 10, 11, 5, 5])
            ffn("b2")
            norm_sum("end2")


def _units(units):
    u = np.stack([np.asarray(v, np.float32) for v in units])
    n, p, c = u.shape
    return np.ascontiguousarray(u.reshape(n // 2, 2, p, c).transpose(0, 2, 1, 3))


def _rows(w):
    k = w.shape[0] // P
    return w.reshape(k, P, -1).transpose(1, 0, 2).reshape(P, -1)


def _columns(w, first, n):
    return [_rows(w[:, first + P * t:first + P * (t + 1)]) for t in range(n)]


def _gain(g):
    return np.asarray(g, np.float32).reshape(-1, P).T


def _features(a):
    return np.ascontiguousarray(a.reshape(a.shape[0], -1, P).transpose(2, 1, 0))


def _constants():
    c = np.zeros((P, N_CONST), np.float32)
    c[:, K_ID:K_ID + P] = np.eye(P)
    c[:, K_ONE:K_ONE + P] = 1.0
    for m in range(P):
        if m % 64 < 32:
            c[m + 32, K_ROT + m] = -1.0
        else:
            c[m - 32, K_ROT + m] = 1.0
    p, j = np.arange(P)[:, None], np.arange(TOK)[None, :]
    c[:, K_MASK1:K_MASK1 + META + P] = np.where(j[:, :META + P] <= META + p, 0.0, NEG)
    c[:, K_MASK1 + META + P:K_MASK1 + N_MASK1] = np.where(j <= META + P + p, 0.0, NEG)
    j = np.arange(SEQ)[None, :]
    c[:, K_MASK2:K_MASK2 + P] = np.where(j[:, :P] // 64 <= p // 64, 0.0, NEG)
    c[:, K_MASK2 + P:K_MASK2 + N_MASK2] = np.where(j // 64 <= (P + p) // 64, 0.0, NEG)
    j, i = np.arange(P)[:, None], np.arange(P)[None, :]
    for level in range(7):
        b = 2 ** level
        c[:, K_LEV + level * P:K_LEV + (level + 1) * P] = (i > j) & (i // (2 * b) == j // (2 * b)) & (i // b != j // b)
    c[:, K_CAUS:K_CAUS + P] = np.where(i >= j, 0.0, NEG)
    return c


def _layout(v):
    v = {n: np.asarray(a) for n, a in v.items()}
    a = {}
    w = v["w_in"][0]
    value = [w[2 * j * P:(2 * j + 2) * P, 2048:2560].reshape(2, P, 512).transpose(1, 0, 2).reshape(P, -1)
             for j in range(4)]
    a["w_in1"] = _units(_columns(w, 1024, 4) + _columns(w, 1536, 4) + value + _columns(w, 2560, 4)
                        + _columns(w, 0, 4) + _columns(w, 512, 4) + _columns(w, 3080, 8) + _columns(w, 4104, 8))
    a["w_pool"] = _units([np.concatenate([v["pool_w"][0][2 * j], v["pool_w"][0][2 * j + 1]], 1) for j in range(2)])
    a["w_up"] = _units([_rows(np.concatenate([v["w_up_pool"][0], v["w_up_attn"][0]], 0)[:, P * m:P * (m + 1)])
                        for m in range(KC)])
    a["w_out1"] = _units(_columns(v["w_out"][0], 0, KC))
    kv = []
    for w in v["w_mem_kv_2"]:
        kv += _columns(w, 0, 2) + [_rows(w[j * 512:(j + 1) * 512, 256:512]) for j in range(2)]
    a["w_memkv"] = _units(kv)
    for which, gu, down in (("a1", v["ffn1_w_gu_2"][0], v["ffn1_w_down_2"][0]),
                            ("a2", v["ffn2_w_gu_2"][0], v["ffn2_w_down_2"][0]),
                            ("b1", v["ffn1_w_gu_2"][1], v["ffn1_w_down_2"][1]),
                            ("b2", v["ffn2_w_gu_2"][1], v["ffn2_w_down_2"][1])):
        g, u = _columns(gu, 0, FT), _columns(gu, FF, FT)
        a["w_gu_" + which] = _units([t for pair in zip(g, u) for t in pair])
        a["w_down_" + which] = _units([_rows(down[j * (FF // 2):(j + 1) * (FF // 2), P * m:P * (m + 1)])
                                       for m in range(KC) for j in range(2)])
    w = v["a_w_in_2"][0]
    a["w_in_a"] = _units(_columns(w, 768, 6) + _columns(w, 0, 6) + _columns(w, 1536, 6)
                         + _columns(w, 3084, 2) + _columns(w, 2304, 6))
    a["w_out_a"] = _units(_columns(v["w_out_2"][0], 0, KC))
    a["w_out_b"] = _units(_columns(v["w_out_2"][1], 0, KC))
    dkv = v["w_dkv_2"]
    a["w_lat"] = _units(_columns(dkv, 0, 2))
    rope = np.concatenate([dkv[:, 256:320]] * 2, 1)
    a["w_krope"] = _units([_rows(rope[j * 512:(j + 1) * 512]) for j in range(2)])
    ukv, uq = v["w_ukv_2"], v["b_w_uq_2"][0]
    a["w_knope"] = _units([np.concatenate([_rows(ukv[:, h * 256:h * 256 + P]) for h in range(3 * j, 3 * j + 3)], 1)
                           for j in range(2)])
    a["w_vmla"] = _units([np.concatenate([ukv[k * P:(k + 1) * P, h * 256 + P:h * 256 + 2 * P] for h in range(6)], 1)
                          for k in range(2)])
    a["w_qnope"] = _units([np.concatenate([_rows(uq[:, h * 192:h * 192 + P]) for h in range(3 * j, 3 * j + 3)], 1)
                           for j in range(2)])
    rope = np.concatenate([_rows(np.concatenate([uq[:, h * 192 + P:(h + 1) * 192] for h in (2 * j, 2 * j + 1)], 1))
                           for j in range(3)], 1)
    a["w_qrope"] = _units([rope[:, 0:3 * P], rope[:, 3 * P:]])
    a["w_in_b"] = _units(_columns(v["b_w_in_2"][0], 0, 4))
    a["x0"] = _features(np.concatenate([v["meta_tokens"], v["x"][0]], 0))
    a["x"] = _features(v["x"][0])
    a["mem"] = _features(v["mem_2"][0])
    a["const"] = _constants()
    par = np.zeros((P, N_PARAM), np.float32)
    gains = {"in1": v["norm_g"][0], "end1": v["final_norm_g"], "mem": v["mem_norm_2"], "ffn_a1": v["ffn1_norm_2"][0],
             "mix_a": v["mix_norm_2"][0], "ffn_a2": v["ffn2_norm_2"][0], "kv": v["kv_in_norm_2"],
             "ffn_b1": v["ffn1_norm_2"][1], "mix_b": v["mix_norm_2"][1], "ffn_b2": v["ffn2_norm_2"][1],
             "end2": v["final_norm_2"]}
    for name, g in gains.items():
        par[:, GAIN[name]:GAIN[name] + KC] = _gain(g)
    par[:, C_POOL:C_POOL + 4] = _gain(v["pool_scale"][0])
    conv = v["a_conv_2"][0]
    for t in range(18):
        first = (768, 0, 1536)[t // 6] + t % 6 * P
        par[:, C_CONV + 4 * t:C_CONV + 4 * t + 4] = conv[:, first:first + P].T
    par[:, C_OUTG] = v["a_out_norm_2"][0]
    par[:, C_QLAT:C_QLAT + 2] = _gain(v["b_q_norm_2"][0])
    par[:, C_KVLAT:C_KVLAT + 2] = _gain(v["kv_lat_norm_2"])
    par[0:8, C_BF] = v["b_forget"][0]
    par[32:38, C_DT] = v["a_dt_bias_2"][0]
    par[32:38, C_ALOG] = v["a_A_log_2"][0]
    inv = (10000.0 ** (-np.arange(0, 64, 2) / 64)).astype(np.float32)
    par[:, C_INV] = np.tile(inv, 4)
    a["par"] = par
    forget = np.zeros((P, 184), np.float32)
    forget[:, 0:64] = _rows(v["w_in"][0][:, 3072:3080])
    a["w_forget"] = forget
    w = np.zeros((D, 38), np.float32)
    w[:, 0:6], w[:, 32:38] = v["a_w_in_2"][0][:, 3072:3078], v["a_w_in_2"][0][:, 3078:3084]
    ba = np.zeros((P, 394), np.float32)
    ba[:, 0:304] = _rows(w)
    a["w_ba"] = ba
    a["pos"] = np.ascontiguousarray(np.broadcast_to(v["positions_2"].reshape(1, SEQ).astype(np.int32), (P, SEQ)))
    return a


def kernel(**inputs):
    import concourse.bacc as bacc
    from concourse.bass_utils import run_bass_kernel_spmd

    nc = bacc.Bacc("TRN2", target_bir_lowering=False, num_devices=1)
    arrays = _layout(inputs)
    dram = {n: nc.dram_tensor("in_" + n, a.shape, mybir.dt.from_np(a.dtype), kind="ExternalInput").ap()
            for n, a in arrays.items()}
    out = nc.dram_tensor("out_0", (KC, P, SEQ), F32, kind="ExternalOutput").ap()
    program(nc, dram, out)
    result = run_bass_kernel_spmd(nc, [{"in_" + n: a for n, a in arrays.items()}], core_ids=[0])
    y = np.asarray(result.results[0]["out_0"])
    return np.ascontiguousarray(y.reshape(D, SEQ).T)[None]
```
